# Optimizing a Trainium2 kernel written in Bass

```python
import jax, jax.numpy as jnp
from jax import lax
import numpy as np

D_MODEL = 1024
BATCH = 1
SEQ = 512
DEPTH = 2

GRID_W = 64
CTX_LEN = 256
N_MIXERS = 2
EXPAND = 2
D_BRANCH = EXPAND * D_MODEL
FNET_GROUPS = 8
FNET_GROUP_DIM = D_BRANCH // FNET_GROUPS
RET_QK_DIM = 256
RET_HEADS = D_MODEL // RET_QK_DIM
RET_V_DIM = D_BRANCH // RET_HEADS
RET_CHUNK = 128
RET_IN_DIM = 2 * RET_HEADS * RET_QK_DIM + 2 * D_BRANCH
ROPE_BASE = 10000.0
EPS = 1e-6
N_FNET_LAYERS = (DEPTH + 1) // 2
N_RET_LAYERS = DEPTH // 2

kernel_name = 'hybrid_fnet_retention_dit_trunk'

def rmsnorm(x, g):
    xf = x.astype(jnp.float32)
    y = xf * lax.rsqrt(jnp.mean(xf * xf, axis=-1, keepdims=True) + EPS) * g.astype(jnp.float32)
    return y.astype(x.dtype)

def ada_params(cond, w, b):
    m = jax.nn.silu(cond) @ w + b
    return jnp.split(m, 3, axis=-1)

def fourier_mixer(h, w_in, w_out):
    b, l, _ = h.shape
    u, z = jnp.split(h @ w_in, 2, axis=-1)
    ug = u.astype(jnp.float32).reshape(b, l, FNET_GROUPS, FNET_GROUP_DIM)
    y = jnp.fft.fft2(ug, axes=(1, 3), norm='ortho').real
    y = y.reshape(b, l, D_BRANCH).astype(h.dtype)
    return (y * jax.nn.silu(z)) @ w_out

def axial_rope(t, row, col):
    half = t.shape[-1] // 2
    nf = half // 2
    freqs = ROPE_BASE ** (-jnp.arange(nf, dtype=jnp.float32) / nf)

    def rot(xp, pos):
        ang = pos[:, None] * freqs[None, :]
        cos = jnp.cos(ang)[None, :, None, :]
        sin = jnp.sin(ang)[None, :, None, :]
        x1, x2 = xp[..., :nf], xp[..., nf:]
        return jnp.concatenate([x1 * cos - x2 * sin, x1 * sin + x2 * cos], axis=-1)

    return jnp.concatenate([rot(t[..., :half], row), rot(t[..., half:], col)], axis=-1)

def ret_projections(h, w_in):
    b, l, _ = h.shape
    hq = RET_HEADS * RET_QK_DIM
    p = h @ w_in
    q, k, v, z = jnp.split(p, [hq, 2 * hq, 2 * hq + D_BRANCH], axis=-1)
    q = q.astype(jnp.float32).reshape(b, l, RET_HEADS, RET_QK_DIM)
    k = k.astype(jnp.float32).reshape(b, l, RET_HEADS, RET_QK_DIM) * (RET_QK_DIM ** -0.5)
    v = v.astype(jnp.float32).reshape(b, l, RET_HEADS, RET_V_DIM)
    return q, k, v, z

def chunk_retention(q, k, v, log_g, r0):
    b, h, l, _ = q.shape
    dv = v.shape[-1]
    n = l // RET_CHUNK
    idx = jnp.arange(RET_CHUNK, dtype=jnp.float32)
    diff = idx[:, None] - idx[None, :]
    dec_intra = jnp.where(diff[None] >= 0.0,
                          jnp.exp(jnp.maximum(diff, 0.0)[None] * log_g[:, None, None]), 0.0)
    dec_cross = jnp.exp((idx + 1.0)[None, :] * log_g[:, None])
    dec_state = jnp.exp((RET_CHUNK - 1.0 - idx)[None, :] * log_g[:, None])
    dec_chunk = jnp.exp(RET_CHUNK * log_g)[:, None, None]

    def to_chunks(t):
        return jnp.moveaxis(t.reshape(b, h, n, RET_CHUNK, t.shape[-1]), 2, 0)

    def step(r, qkv):
        qc, kc, vc = qkv
        s = jnp.einsum('bhjd,bhmd->bhjm', qc, kc) * dec_intra
        o = (jnp.einsum('bhjm,bhme->bhje', s, vc)
             + jnp.einsum('bhjd,bhde->bhje', qc, r) * dec_cross[..., None])
        r = dec_chunk * r + jnp.einsum('bhmd,bhme->bhde', kc * dec_state[..., None], vc)
        return r, o

    r, o = lax.scan(step, r0, (to_chunks(q), to_chunks(k), to_chunks(v)))
    o = jnp.moveaxis(o, 0, 2).reshape(b, h, l, dv)
    return o, r

def bi_retention(q, k, v, log_g_f, log_g_b, r0_f, r0_b):
    o_f, r_f = chunk_retention(q, k, v, log_g_f, r0_f)
    flip = lambda t: jnp.flip(t, axis=2)
    o_b, r_b = chunk_retention(flip(q), flip(k), flip(v), log_g_b, r0_b)
    return o_f + flip(o_b), r_f, r_b

def ret_output(o, z, w_out):
    b, h, l, dv = o.shape
    o = o * lax.rsqrt(jnp.mean(o * o, axis=-1, keepdims=True) + EPS)
    o = jnp.transpose(o, (0, 2, 1, 3)).reshape(b, l, h * dv).astype(z.dtype)
    return (o * jax.nn.silu(z)) @ w_out

def retention_mixer(h_lat, h_ctx, w_in, w_out, decay, row, col, need_ctx_out):
    log_g = jnp.log1p(-jnp.exp2(decay.astype(jnp.float32)))
    ql, kl, vl, zl = ret_projections(h_lat, w_in)
    qc, kc, vc, zc = ret_projections(h_ctx, w_in)
    ql = axial_rope(ql, row, col)
    kl = axial_rope(kl, row, col)
    tr = lambda t: jnp.transpose(t, (0, 2, 1, 3))
    b = h_lat.shape[0]
    zeros = jnp.zeros((b, RET_HEADS, RET_QK_DIM, RET_V_DIM), jnp.float32)
    oc, r_f, r_b = bi_retention(tr(qc), tr(kc), tr(vc), log_g[0], log_g[1], zeros, zeros)
    ol, _, _ = bi_retention(tr(ql), tr(kl), tr(vl), log_g[0], log_g[1], r_f, r_b)
    out_lat = ret_output(ol, zl, w_out)
    out_ctx = ret_output(oc, zc, w_out) if need_ctx_out else None
    return out_lat, out_ctx

def setup_inputs(seed: int = 0) -> dict:
    key = jax.random.key(seed)
    ks = jax.random.split(key, 16)
    f32 = jnp.float32
    nrm = lambda k, s: jax.random.normal(k, s, f32)
    return {
        'x': nrm(ks[0], (BATCH, SEQ, D_MODEL)),
        'c': nrm(ks[1], (BATCH, D_MODEL)),
        'ctx': nrm(ks[2], (BATCH, CTX_LEN, D_MODEL)),
        'c_ctx': nrm(ks[3], (D_MODEL,)),
        'norm_g': 1.0 + 0.02 * nrm(ks[4], (DEPTH, D_MODEL)),
        'ada_w': nrm(ks[5], (DEPTH, D_MODEL, 3 * D_MODEL)) * (0.5 * D_MODEL ** -0.5),
        'ada_b': 0.01 * nrm(ks[6], (DEPTH, 3 * D_MODEL)),
        'fnet_w_in': nrm(ks[7], (N_FNET_LAYERS, D_MODEL, 2 * D_BRANCH)) * D_MODEL ** -0.5,
        'fnet_w_out': nrm(ks[8], (N_FNET_LAYERS, D_BRANCH, D_MODEL)) * D_BRANCH ** -0.5,
        'ret_w_in': nrm(ks[9], (N_RET_LAYERS, D_MODEL, RET_IN_DIM)) * D_MODEL ** -0.5,
        'ret_w_out': nrm(ks[10], (N_RET_LAYERS, D_BRANCH, D_MODEL)) * D_BRANCH ** -0.5,
        'ret_decay': (-5.0 - jnp.arange(RET_HEADS, dtype=f32))[None, None, :]
                     + 0.1 * nrm(ks[11], (N_RET_LAYERS, 2, RET_HEADS)),
        'final_g': 1.0 + 0.02 * nrm(ks[12], (D_MODEL,)),
    }

def reference(x, c, ctx, c_ctx, norm_g, ada_w, ada_b, fnet_w_in, fnet_w_out,
              ret_w_in, ret_w_out, ret_decay, final_g):
    n_lat = x.shape[1]
    rows = n_lat // GRID_W
    pos = jnp.arange(rows * GRID_W)
    row = (pos // GRID_W).astype(jnp.float32)
    col = (pos % GRID_W).astype(jnp.float32)
    for i in range(DEPTH):
        last = i == DEPTH - 1
        sh_l, sc_l, gt_l = ada_params(c, ada_w[i], ada_b[i])
        sh_c, sc_c, gt_c = ada_params(c_ctx, ada_w[i], ada_b[i])
        hl = rmsnorm(x, norm_g[i]) * (1.0 + sc_l[:, None, :]) + sh_l[:, None, :]
        hc = rmsnorm(ctx, norm_g[i]) * (1.0 + sc_c) + sh_c
        j = i // N_MIXERS
        if i % N_MIXERS == 0:
            ol = fourier_mixer(hl, fnet_w_in[j], fnet_w_out[j])
            oc = None if last else fourier_mixer(hc, fnet_w_in[j], fnet_w_out[j])
        else:
            ol, oc = retention_mixer(hl, hc, ret_w_in[j], ret_w_out[j], ret_decay[j],
                                     row, col, not last)
        x = x + gt_l[:, None, :] * ol
        if not last:
            ctx = ctx + gt_c * oc
    return rmsnorm(x, final_g)


_drawn_inputs = setup_inputs


def setup_inputs(seed=0):
    import zlib

    import numpy as np

    out = dict(_drawn_inputs(seed))
    spreads = {}
    factors = {'norm_g': 6.865, 'ada_b': 4.977, 'final_g': 2.888}
    for name, (base, spread) in spreads.items():
        noise = np.random.default_rng([zlib.crc32(name.encode()), seed]).standard_normal(out[name].shape)
        drawn = base * np.exp(spread * noise) if base else spread * noise
        out[name] = __import__('jax').numpy.asarray(drawn.astype(out[name].dtype))
    for name, factor in factors.items():
        out[name] = (out[name] * factor).astype(out[name].dtype)
    return out
```

```python
from contextlib import ExitStack

import numpy as np

import concourse.bass as bass
from concourse import mybir

F32 = mybir.dt.float32
F32R = mybir.dt.float32r
I32 = mybir.dt.int32
ALU = mybir.AluOpType
ACT = mybir.ActivationFunctionType

P = 128
D = 1024
KT = D // P
LAT, CTX = 512, 256
TOK = LAT + CTX
TT = TOK // P
DB = 2048
FT = DB // P
GROUPS, GDIM = 8, 256
HEADS, QK, DV = 4, 256, 512
GRID_W = 64
ROPE_BASE = 10000.0
EPS = 1e-6
HALF = LAT // 2 + 1
NB = HALF + 1
AB = GDIM + 2
SLOT = 1024

Z_PER, Z_ITERS = 6, 8
SLOT_U = Z_PER * Z_ITERS
SLOT_OUT0 = SLOT_U + 2 * GROUPS
SLOT_HEAD = SLOT_OUT0 + 2 * KT
HEAD_PER = 12
SLOT_OUT1 = SLOT_HEAD + HEAD_PER * HEADS
SLOTS = SLOT_OUT1 + 2 * KT
RAW_BUFS = 3
V_BANK = (2, 3, 4, 5, 0, 1)
POOL_TILES = 3
DONE0 = 2
SPLIT0 = 3

PHASES = {
    "gate": (0, 3, (0, 0, 0)),
    "fnet": (SLOT_U, 2, (16, 16, 16)),
    "head": (SLOT_HEAD, 3, (32, 32, 16)),
    "out1": (SLOT_OUT1, 2, (48, 48, 32)),
}


def raw_at(phase, n):
    _, bufs, before = PHASES[phase]
    return n % bufs, 16 * (before[n % bufs] + n // bufs + 1)


def raw_step(phase, per_iteration):
    return 16 * (per_iteration // PHASES[phase][1])


def split_table(table):
    full = table.astype(np.float32)
    bits = full.view(np.uint32).astype(np.uint64)
    hi = ((bits + 0x800) & 0xFFFFF000).astype(np.uint32).view(np.float32)
    lo = (table - hi.astype(np.float64)).astype(np.float32)
    return hi, lo


def dft_tables():
    p = np.arange(P)[:, None, None]

    def phase(tiles, cols, n):
        rows = p + P * np.arange(tiles)[None, :, None]
        return 2 * np.pi * ((rows * np.asarray(cols)[None, None, :]) % n) / n

    k = np.arange(P)
    feat = np.concatenate([np.cos(phase(2, k, GDIM)), np.sin(phase(2, k, GDIM)),
                           np.cos(phase(2, [P], GDIM)), np.zeros((P, 2, 1))], 2) / np.sqrt(GDIM)
    lat_cos = np.cos(phase(4, np.arange(NB), LAT)) / np.sqrt(LAT)
    lat_sin = np.sin(phase(4, np.arange(LAT // 2), LAT)) / np.sqrt(LAT)
    ctx_cos = np.cos(phase(2, np.arange(CTX), CTX)) / np.sqrt(CTX)
    ctx_sin = np.sin(phase(2, np.arange(CTX), CTX)) / np.sqrt(CTX)
    parts = []
    for t in (feat, lat_cos, lat_sin, ctx_cos, ctx_sin):
        for half in split_table(t.reshape(P, -1)):
            parts.append(half)
    return np.ascontiguousarray(np.concatenate(parts, 1))


def rope_tables():
    nf = QK // 4
    freqs = ROPE_BASE ** (-np.arange(nf, dtype=np.float32) / np.float32(nf))
    pos = np.arange(LAT)
    ang = np.concatenate([freqs[:, None] * (pos // GRID_W)[None, :].astype(np.float32),
                          freqs[:, None] * (pos % GRID_W)[None, :].astype(np.float32)], 0)
    return np.ascontiguousarray(np.concatenate([np.cos(ang), np.sin(ang)], 1).astype(np.float32))


TABLE_COLS = 2 * (2 * AB + 4 * NB + 4 * (LAT // 2) + 2 * CTX + 2 * CTX)


def build(nc, x_lat, x_ctx, small_in, decay_in, ada_first, stream, tables_in, rope_in, out):
    ctx = ExitStack()
    with ctx:
        def sb(name, shape, dt=F32):
            return ctx.enter_context(nc.sbuf_tensor(name, shape, dt))

        def sem(name):
            return ctx.enter_context(nc.semaphore(name))

        ring = sb("ring", [P, 2, 2, SLOT], F32R)
        hreg = sb("hreg", [P, 2 * KT * TOK], F32R)
        WREG = 13456
        wreg = sb("wreg", [P, WREG], F32R)
        cond = sb("cond", [P, KT, 4], F32R)
        xl = sb("xl", [P, KT * LAT])
        xc = sb("xc", [P, KT * CTX])
        gate = sb("gate", [P, FT * TOK])
        raw = sb("raw", [P, RAW_BUFS, SLOT])
        small = sb("small", [P, 88])
        csf = sb("csf", [P, 2 * KT])
        mod_t = sb("mod_t", [P, 32, 4])
        mod0 = sb("mod0", [P, 16, 2])
        mod1 = sb("mod1", [P, 32, 2])
        amul = sb("amul", [P, 2, KT, 2])
        ones = sb("ones", [P, P])
        ident4 = sb("ident4", [4, 4])
        eps = sb("eps", [P, 1])
        dk = sb("dk", [P, 10, 8])
        dki = sb("dki", [P, 8], I32)
        dist = sb("dist", [P, 896])
        banks = ctx.enter_context(nc.psum_tensor("banks", [P, 8 * 512], F32))

        def bank(b, n=512, off=0, parts=P):
            return banks[0:parts, 512 * b + off:512 * b + off + n]

        def f32(ap):
            return ap.bitcast(F32)

        def one(ap, i):
            return ap[:, bass.ds(i, 1), :].rearrange("p a n -> p (a n)")

        h_hi = hreg[:, 0:KT * TOK].rearrange("p (k t) -> p k t", k=KT)
        h_lo = hreg[:, KT * TOK:2 * KT * TOK].rearrange("p (k t) -> p k t", k=KT)
        ada_raw = gate[:, 0:4 * 2048].rearrange("p (b n) -> p b n", b=4)
        ada_split = hreg[:, 0:3 * 4096].rearrange("p (b s n) -> p b s n", b=3, s=2)
        rows0 = gate[0:4, 0:2048]
        rows1 = xl[0:4, 0:4096]
        TAIL = 8192
        sq_t = gate[:, TAIL:TAIL + 2 * TOK].rearrange("p (b n) -> p b n", b=2)
        cos_t = gate[:, TAIL + 1536:TAIL + 2048]
        sin_t = gate[:, TAIL + 2048:TAIL + 2560]
        acc_t = gate[:, TAIL + 2560:TAIL + 2560 + TOK]
        rstd_t = gate[:, TAIL + 3328:TAIL + 3328 + TOK]
        tmp_t = gate[:, 0:KT * TOK].rearrange("p (k t) -> p k t", k=KT)
        gate0 = gate[:, :].rearrange("p (f t) -> p f t", f=FT)
        gate1 = gate[:, 0:FT * LAT].rearrange("p (f t) -> p f t", f=FT)
        x3 = xl[:, :].rearrange("p (k t) -> p k t", k=KT)
        xc3 = xc[:, :].rearrange("p (k t) -> p k t", k=KT)

        tables = wreg[:, 0:TABLE_COLS]
        at = [0]

        def take(a, b):
            v = wreg[:, at[0]:at[0] + a * b].rearrange("p (a b) -> p a b", a=a)
            at[0] += a * b
            return v

        feat = [take(2, AB), take(2, AB)]
        lat_cos = [take(4, NB), take(4, NB)]
        lat_sin = [take(4, LAT // 2), take(4, LAT // 2)]
        ctx_cos = [take(2, CTX), take(2, CTX)]
        ctx_sin = [take(2, CTX), take(2, CTX)]
        assert at[0] == TABLE_COLS
        u = [take(2, TOK), take(2, TOK)]
        ab = [take(TT, AB), take(TT, AB)]
        nyq = [take(TT, GROUPS), take(TT, GROUPS)]
        assert at[0] <= WREG
        d_lat, s_lat, q_lat = xc[:, 0:NB], xc[:, NB:2 * NB], xc[:, 2 * NB:3 * NB]
        d_ctx, s_ctx, q_ctx = (xc[:, 3 * NB + CTX * i:3 * NB + CTX * (i + 1)] for i in range(3))
        nyq_gate = xl[0:GROUPS, 0:TOK]
        nyq_y = xl[0:GROUPS, TOK:2 * TOK]

        def g0(kk, part):
            r = hreg if kk < 8 else wreg
            o = (kk % 8) * 2 * TOK + part * TOK
            return r[:, o:o + TOK]

        def g1(kk, part):
            r = hreg if kk < 12 else wreg
            o = (kk % 12) * 2 * LAT + part * LAT
            return r[:, o:o + LAT]

        at[0] = 0
        q_s = [take(2, LAT), take(2, LAT)]
        k_s = [take(2, TOK), take(2, TOK)]
        v_s = [take(TT, DV), take(TT, DV)]
        p_s = [take(2, LAT), take(2, LAT)]
        assert at[0] <= WREG
        turn = [xc[:, 512 * i:512 * (i + 1)] for i in range(4)]
        dexp = xc[:, 0:896]
        strip_lat = gate[:, TAIL:TAIL + 896]
        strip_ctx = gate[:, TAIL + 896:TAIL + 1536]
        p_f = gate[:, TAIL + 2560:TAIL + 3584].rearrange("p (b n) -> p b n", b=2)
        head_rstd = gate[:, TAIL + 3584:TAIL + 4096]

        g_norm = [small[:, 16:24], small[:, 24:32]]
        g_final = small[:, 32:40]
        bias0, bias1 = small[:, 40:64], small[:, 64:88]
        log_g = dk[:, 9, :]
        neg_lb = dk[:, 8, 4:8]

        s_small, s_decay, s_xl, s_xc = sem("small_in"), sem("decay_in"), sem("xl_in"), sem("xc_in")
        s_ada = [sem(f"ada_in{i}") for i in range(4)]
        s_raw = [sem(f"raw_in{i}") for i in range(RAW_BUFS)]
        s_tables, s_rope, s_out = sem("tables_in"), sem("rope_in"), sem("out_stored")
        s_xl2, s_xc2 = sem("xl_again"), sem("xc_again")
        s_nyqg, s_nyqs = sem("nyq_gate_in"), sem("nyq_stored")
        ones_set, ident_set, eps_set = sem("ones_set"), sem("ident_set"), sem("eps_set")
        hi_done, split_done, slot_done = sem("hi_done"), sem("split_done"), sem("slot_done")
        csf_done, cond_done = sem("csf_done"), sem("cond_done")
        sq_done, sum_sq_done = sem("sq_done"), sem("sum_sq_done")
        root_done, rstd_done = sem("root_done"), sem("rstd_done")
        ada_hi, ada_lo, ada_mm = sem("ada_hi"), sem("ada_lo"), sem("ada_mm")
        rows0_done, mod0_tr, mods = sem("rows0_done"), sem("mod0_tr"), sem("mods_done")
        t_vec, t_pool = sem("t_vec"), sem("t_pool")
        hf_done, hhi_done, hlo_done = sem("hf_done"), sem("h_hi_done"), sem("h_lo_done")
        z_done, rows_done, mod1_tr = sem("z_done"), sem("rows_done"), sem("mod1_tr")
        uhi, ulo = sem("u_hi_done"), sem("u_lo_done")
        feat_done, abhi, ablo = sem("feat_done"), sem("ab_hi_done"), sem("ab_lo_done")
        seq_done, q_copied, ds_done = sem("seq_done"), sem("q_copied"), sem("ds_done")
        gated, nyq_copied = sem("gated"), sem("nyq_copied")
        nyq_mm, nyq_vec = sem("nyq_mm"), sem("nyq_vec")
        ghi, glo = sem("g_hi_done"), sem("g_lo_done")
        x1_done, acc_done = sem("x1_done"), sem("acc_done")
        step, rest_done, ln_done = sem("vector_step"), sem("rest_done"), sem("ln_done")
        turned, summed = sem("turned"), sem("turn_summed")
        qkhi, qklo = sem("qk_hi_done"), sem("qk_lo_done")
        z1_done, vhi, vlo = sem("z1_done"), sem("v_hi_done"), sem("v_lo_done")
        dist_set, expo_done, exp_done = sem("dist_set"), sem("expo_done"), sem("exp_done")
        strip_done = sem("strip_done")
        score_done, pf_done, phi, plo = (sem("score_done"), sem("p_f_done"), sem("p_hi_done"),
                                         sem("p_lo_done"))
        pv_done = sem("pv_done")
        osq, oacc, oss = sem("o_sq_done"), sem("o_acc_done"), sem("o_sum_sq_done")
        oroot, orstd, onorm, ogated = (sem("o_root_done"), sem("o_rstd_done"), sem("o_norm_done"),
                                       sem("o_gated"))
        gained, out_vec, out_pool = sem("gained"), sem("out_vec"), sem("out_pool")

        block = ctx.enter_context(nc.Block())


        @block.sync
        def _(sp):
            def load_slot(t, buf, free_at):
                sp.wait_ge(split_done, free_at)
                sp.dma_start(raw[:, buf, :], stream[t]).then_inc(s_raw[buf], 16)

            sp.dma_start(small[:, :], small_in).then_inc(s_small, 16)
            sp.dma_start(dk[:, 0, :], decay_in.partition_broadcast(P)).then_inc(s_decay, 16)
            sp.dma_start(xl[:, :], x_lat).then_inc(s_xl, 16)
            sp.dma_start(xc[:, :], x_ctx).then_inc(s_xc, 16)
            for k in range(KT):
                if k >= 4:
                    sp.wait_ge(ada_lo, k - 3)
                sp.dma_start(ada_raw[:, k % 4, :], ada_first[k]).then_inc(s_ada[k % 4], 16)
            with sp.Fori(0, Z_ITERS) as j:
                for s in range(Z_PER):
                    load_slot(Z_PER * j + s, s % 3, Z_PER * j + s + 1 - 3 + SPLIT0)
            with sp.Fori(0, GROUPS + KT) as j:
                for s in range(2):
                    load_slot(2 * j + SLOT_U + s, s, 2 * j + SLOT_U + s + 1 - 2 + SPLIT0)
            sp.wait_ge(split_done, SLOT_HEAD + SPLIT0)
            with sp.Fori(0, HEADS) as h:
                for s in range(HEAD_PER):
                    t = HEAD_PER * h + (SLOT_HEAD + s)
                    load_slot(t, s % 3, HEAD_PER * h + (SLOT_HEAD + s + 1 - 3 + SPLIT0))
            with sp.Fori(0, KT) as j:
                for s in range(2):
                    load_slot(2 * j + SLOT_OUT1 + s, s, 2 * j + SLOT_OUT1 + s + 1 - 2 + SPLIT0)
            for m in range(KT):
                if m < POOL_TILES:
                    sp.wait_ge(out_pool, m + 1)
                    src = tmp_t[:, m, 0:LAT]
                else:
                    sp.wait_ge(out_vec, m - POOL_TILES + 1)
                    src = x3[:, m, :]
                sp.dma_start(out[m], src).then_inc(s_out, 16)
            sp.wait_ge(s_out, 16 * KT)

        @block.gpsimd
        def _(pool):
            pool.sem_inc(gated, 6)
            pool.memset(ones[:, :], 1.0).then_inc(ones_set, 1)
            pool.memset(ident4[:, :], 0.0).then_inc(ident_set, 1)
            pool.wait_ge(ident_set, 1)
            pool.affine_select(out=ident4[:, :], in_=ident4[:, :], compare_op=ALU.not_equal,
                               fill=1.0, base=0, pattern=[[-1, 4]],
                               channel_multiplier=1).then_inc(ident_set, 1)
            pool.iota(dist[:, :], pattern=[[1, 896]], base=-384, channel_multiplier=-1,
                      allow_small_or_imprecise_dtypes=True).then_inc(dist_set, 1)
            pool.wait_ge(rstd_done, 1)
            for k in range(KT):
                pool.tensor_tensor(x3[:, k, :], x3[:, k, :], rstd_t[:, 0:LAT],
                                   ALU.mult).then_inc(t_pool, 1)
                pool.tensor_tensor(xc3[:, k, :], xc3[:, k, :], rstd_t[:, LAT:TOK],
                                   ALU.mult).then_inc(t_pool, 1)
            pool.wait_ge(ada_lo, KT)
            pool.dma_start(tables, tables_in).then_inc(s_tables, 16)
            pool.wait_ge(z_done, FT + 2)
            pool.wait_ge(mod1_tr, 1)
            pool.dma_start(nyq_gate, gate0[0:1, 8:16, :]).then_inc(s_nyqg, 16)
            pool.wait_ge(s_nyqg, 16)

            def mix_group(p):
                pool.wait_ge(ablo, 6 * p + 6 + 1)
                for part in range(2):
                    pool.tensor_copy(nyq[part][:, :, bass.ds(p, 1)],
                                     f32(ab[part][:, :, GDIM:GDIM + 1])).then_inc(nyq_copied, 1)
                lo, mid = 0, HALF
                pool.wait_ge(ds_done, 4 * p + 2 + 4)
                for f, src, a, b in ((p, d_lat, lo, mid), (p + 8, d_lat, mid, LAT),
                                     (p + 8, s_lat, lo, mid), (p, s_lat, mid, LAT)):
                    y = src[:, 0:HALF] if a == 0 else src[:, LAT // 2 - 1:0:-1]
                    g = one(gate0[:, :, a:b], f)
                    pool.tensor_tensor(g, y, g, ALU.mult).then_inc(gated, 1)
                pool.wait_ge(ds_done, 4 * p + 4 + 4)
                for f, src in ((p, d_ctx), (p + 8, s_ctx)):
                    g = one(gate0[:, :, LAT:TOK], f)
                    pool.tensor_tensor(g, src, g, ALU.mult).then_inc(gated, 1)

            with pool.Fori(0, GROUPS) as p:
                mix_group(p)
            pool.wait_ge(gated, 6 * GROUPS + 6)
            pool.wait_ge(nyq_vec, 4)
            pool.dma_start(gate0[0:1, 8:16, :], nyq_y).then_inc(s_nyqs, 16)
            pool.wait_ge(s_nyqs, 16)
            pool.dma_start(xl[:, :], x_lat).then_inc(s_xl2, 16)
            pool.dma_start(xc[:, :], x_ctx).then_inc(s_xc2, 16)
            pool.wait_ge(glo, FT)
            pool.dma_start(gate[:, TAIL + 1536:TAIL + 2560], rope_in).then_inc(s_rope, 16)
            pool.wait_ge(rstd_done, 2)
            for k in (2, 5):
                pool.tensor_tensor(tmp_t[:, k, 0:LAT], x3[:, k, :], rstd_t[:, 0:LAT],
                                   ALU.mult).then_inc(t_pool, 1)
                pool.tensor_tensor(tmp_t[:, k, LAT:TOK], xc3[:, k, :], rstd_t[:, LAT:TOK],
                                   ALU.mult).then_inc(t_pool, 1)

            def norm_head(h):
                for i in range(1, 4):
                    pool.wait_ge(osq, 4 * h + i + 1)
                    if i > 1:
                        pool.wait_ge(oacc, 3 * h + i - 1)
                    pool.tensor_tensor(head_rstd, head_rstd, p_f[:, i % 2, :],
                                       ALU.add).then_inc(oacc, 1)

            def gate_head(h):
                for i in range(4):
                    pool.wait_ge(onorm, 4 * h + i + 1)
                    g = one(gate1, 4 * h + i)
                    pool.tensor_tensor(g, g, p_f[:, i % 2, :], ALU.mult).then_inc(ogated, 1)

            def head(h, first):
                if not first:
                    norm_head(h - 1)
                def sums(n):
                    pool.wait_ge(turned, 8 * h + 4 * n + 4)
                    pool.tensor_tensor(turn[0], turn[0], turn[1],
                                       ALU.subtract).then_inc(summed, 1)
                    pool.tensor_tensor(turn[2], turn[2], turn[3], ALU.add).then_inc(summed, 1)
                sums(0)
                if not first:
                    gate_head(h - 1)
                sums(1)

            head(0, True)
            with pool.Fori(1, HEADS) as h:
                head(h, False)
            norm_head(HEADS - 1)
            gate_head(HEADS - 1)
            pool.wait_ge(rstd_done, 3)
            for m in range(POOL_TILES):
                pool.wait_ge(gained, m + 1)
                pool.tensor_tensor(tmp_t[:, m, 0:LAT], tmp_t[:, m, 0:LAT], rstd_t[:, 0:LAT],
                                   ALU.mult).then_inc(out_pool, 1)

        @block.scalar
        def _(act):
            def hi(phase, n, t, i=0, per=0):
                buf, landed = raw_at(phase, n)
                act.wait_ge(s_raw[buf], landed + raw_step(phase, per) * i if per else landed)
                act.wait_ge(slot_done, t - 2 + 1 + DONE0)
                act.activation(ring[:, n % 2, 0, :], raw[:, buf, :], ACT.Copy).then_inc(hi_done, 1)

            def h_tiles(layer, src_l, src_c):
                mod = (mod0, mod1)[layer]
                sh = 0 if layer == 0 else 8
                for k in range(KT):
                    pool_tile = layer == 0 or k in (2, 5)
                    if layer == 0:
                        act.wait_ge(t_pool, 2 * k + 2)
                    elif pool_tile:
                        act.wait_ge(t_pool, 16 + (2 if k == 2 else 4))
                    else:
                        act.wait_ge(t_vec, 2 * [0, 1, 3, 4, 6, 7].index(k) + 2)
                    for c, (a, b) in enumerate(((0, LAT), (LAT, TOK))):
                        src = (src_l, src_c)[c][:, k, :] if layer == 0 else tmp_t[:, k, a:b]
                        act.activation(tmp_t[:, k, a:b], src, ACT.Identity,
                                       bias=mod[:, sh + k, c:c + 1],
                                       scale=amul[:, layer, k, c:c + 1]).then_inc(hf_done, 1)
                    act.wait_ge(hf_done, 16 * layer + 2 * k + 2)
                    act.activation(h_hi[:, k, :], tmp_t[:, k, :], ACT.Copy).then_inc(hhi_done, 1)

            act.sem_inc(z_done, 2)
            act.wait_ge(s_small, 16)
            act.activation(csf[:, :], small[:, 0:16], ACT.Silu).then_inc(csf_done, 1)
            act.wait_ge(rest_done, 1)
            act.activation(dk[:, 7, :], dk[:, 7, :], ACT.Ln).then_inc(ln_done, 1)
            act.wait_ge(s_xl, 16)
            act.wait_ge(s_xc, 16)
            for k in range(KT):
                if k >= 2:
                    act.wait_ge(sum_sq_done, k - 1)
                act.activation(sq_t[:, k % 2, 0:LAT], x3[:, k, :], ACT.Square).then_inc(sq_done, 1)
                act.activation(sq_t[:, k % 2, LAT:TOK], xc3[:, k, :],
                               ACT.Square).then_inc(sq_done, 1)
            act.wait_ge(sum_sq_done, KT)
            act.wait_ge(eps_set, 1)
            act.activation(rstd_t, banks[:, 4 * 512:4 * 512 + TOK], ACT.Sqrt, scale=1.0 / D,
                           bias=eps[:, :]).then_inc(root_done, 1)
            for k in range(KT):
                act.wait_ge(s_ada[k % 4], 16 * (k // 4 + 1))
                if k >= 3:
                    act.wait_ge(ada_mm, k - 2)
                act.activation(ada_split[:, k % 3, 0, :], ada_raw[:, k % 4, :],
                               ACT.Copy).then_inc(ada_hi, 1)
            hi("gate", 0, 0)
            act.wait_ge(mods, 1)
            h_tiles(0, x3, xc3)

            with act.Fori(0, Z_ITERS) as j:
                for s in range(Z_PER):
                    hi("gate", s + 1, Z_PER * j + s + 1, j, Z_PER)
                    if s in (1, 4):
                        act.wait_ge(slot_done, Z_PER * j + s - 1 + 1 + DONE0)
                        b = 0 if s == 1 else 2
                        act.activation(one(gate0, 2 * j + s // 4), banks[:, 512 * b:512 * b + TOK],
                                       ACT.Silu).then_inc(z_done, 1)

            def u_hi(g, tile):
                act.wait_ge(slot_done, 2 * g + SLOT_U + tile + 1 + DONE0)
                act.activation(u[0][:, tile, :], banks[:, 1024 * tile:1024 * tile + TOK],
                               ACT.Copy).then_inc(uhi, 1)

            def ab_hi(p):
                act.wait_ge(nyq_copied, 2 * p + 2)
                for t in range(TT):
                    act.wait_ge(feat_done, 6 * p + t + 1)
                    act.activation(ab[0][:, t, :], bank(4 + t % 2, AB), ACT.Copy).then_inc(abhi, 1)

            def copy_q(p):
                act.wait_ge(seq_done, 2 * p + 1)
                act.activation(q_lat[:, 0:LAT // 2], bank(7, LAT // 2),
                               ACT.Copy).then_inc(q_copied, 1)
                act.wait_ge(seq_done, 2 * p + 2)
                act.activation(q_ctx, bank(4, CTX, CTX), ACT.Copy).then_inc(q_copied, 1)

            act.sem_inc(nyq_copied, 2)
            hi("fnet", 1, SLOT_U + 1)
            u_hi(0, 0)
            hi("fnet", 2, SLOT_U + 2)
            u_hi(0, 1)
            with act.Fori(1, GROUPS) as g:
                hi("fnet", 1, 2 * g + SLOT_U + 1, g, 2)
                ab_hi(g - 1)
                u_hi(g, 0)
                hi("fnet", 2, 2 * g + SLOT_U + 2, g, 2)
                u_hi(g, 1)
                copy_q(g - 1)

            def g_hi(kk):
                if kk < 8:
                    act.wait_ge(gated, 6 * (kk + 1) + 6)
                else:
                    act.wait_ge(s_nyqs, 16)
                act.activation(g0(kk, 0), gate0[:, kk, :], ACT.Copy).then_inc(ghi, 1)

            hi("fnet", 2 * GROUPS + 1, SLOT_OUT0 + 1)
            ab_hi(GROUPS - 1)
            for kk in range(4):
                g_hi(kk)
            copy_q(GROUPS - 1)
            for kk in range(4, FT):
                g_hi(kk)

            with act.Fori(0, KT) as m:
                hi("fnet", 2 * GROUPS + 2, 2 * m + SLOT_OUT0 + 2, m, 2)
                hi("fnet", 2 * GROUPS + 3, 2 * m + SLOT_OUT0 + 3, m, 2)
                act.wait_ge(x1_done, 2 * m + (2 + 4))
                act.wait_ge(acc_done, m + 1)
                act.activation(sq_t[:, 0, 0:LAT], one(x3, m), ACT.Square).then_inc(sq_done, 1)
                act.activation(sq_t[:, 0, LAT:TOK], one(xc3, m), ACT.Square).then_inc(sq_done, 1)
            act.wait_ge(mods, 2)
            act.wait_ge(sum_sq_done, KT + 1)
            act.activation(rstd_t, banks[:, 4 * 512:4 * 512 + TOK], ACT.Sqrt, scale=1.0 / D,
                           bias=eps[:, :]).then_inc(root_done, 1)
            h_tiles(1, x3, xc3)

            def o_squares(h):
                for i in range(4):
                    act.wait_ge(pv_done, 6 * h + 6)
                    if i == 3:
                        act.wait_ge(oacc, 3 * h + 1)
                    dst = head_rstd if i == 0 else p_f[:, i % 2, :]
                    act.activation(dst, bank(2 + i), ACT.Square).then_inc(osq, 1)

            def o_root(h):
                act.wait_ge(oss, h + 1)
                act.activation(head_rstd, bank(6), ACT.Sqrt, scale=1.0 / DV,
                               bias=eps[:, :]).then_inc(oroot, 1)

            def g1_hi(kk):
                if kk >= 12:
                    act.wait_ge(ogated, kk + 1)
                act.activation(g1(kk, 0), gate1[:, kk, :], ACT.Copy).then_inc(ghi, 1)

            def head(h, first=False, last=False):
                def used(s):
                    hi("head", s + 2, HEAD_PER * h + (SLOT_HEAD + s + 2), h, HEAD_PER)

                def turned_hi(n, dst):
                    for i in range(2):
                        act.wait_ge(summed, 4 * h + 2 * n + i + 1)
                        act.activation(dst[:, i, 0:LAT], turn[2 * i],
                                       ACT.Copy).then_inc(qkhi, 1)

                def silu(i, b):
                    act.activation(one(gate1, 4 * h + i), bank(b), ACT.Silu).then_inc(z1_done, 1)

                used(0)
                used(1)
                turned_hi(0, q_s[0])
                if not first:
                    o_root(h - 1)
                used(2)
                silu(0, 7)
                used(3)
                silu(1, 6)
                used(4)
                act.activation(k_s[0][:, 0, LAT:TOK], bank(3, CTX), ACT.Copy).then_inc(qkhi, 1)
                used(5)
                act.activation(k_s[0][:, 1, LAT:TOK], bank(5, CTX), ACT.Copy).then_inc(qkhi, 1)
                turned_hi(1, k_s[0])
                used(6)
                silu(2, 7)
                used(7)
                act.wait_ge(expo_done, 5 * h + 2)
                act.activation(strip_ctx, strip_ctx, ACT.Exp).then_inc(exp_done, 1)
                act.activation(dexp[:, 0:640], dexp[:, 0:640], ACT.Exp).then_inc(exp_done, 1)
                used(8)
                act.wait_ge(expo_done, 5 * h + 5)
                act.activation(strip_lat, strip_lat, ACT.Exp).then_inc(exp_done, 1)
                used(9)
                used(10)
                for t in range(TT):
                    act.activation(v_s[0][:, t, :], bank(V_BANK[t]), ACT.Copy).then_inc(vhi, 1)
                used(11)
                silu(3, 7)
                if last:
                    act.wait_ge(ogated, 12)
                for t in range(TT):
                    act.wait_ge(pf_done, 6 * h + t + 1)
                    if t >= 2:
                        act.wait_ge(pv_done, 6 * h + t - 1)
                    act.activation(p_s[0][:, t % 2, :], p_f[:, t % 2, :],
                                   ACT.Copy).then_inc(phi, 1)
                    if last:
                        g1_hi(2 * t)
                        g1_hi(2 * t + 1)

            head(0, first=True)
            with act.Fori(1, HEADS - 1) as h:
                o_squares(h - 1)
                head(h)
            o_squares(HEADS - 2)
            head(HEADS - 1, last=True)
            o_squares(HEADS - 1)
            o_root(HEADS - 1)
            for kk in range(12, FT):
                g1_hi(kk)

            def x2_sq(m):
                act.wait_ge(x1_done, m + (2 * KT + 1 + 4))
                act.wait_ge(acc_done, m + (KT + 2))
                act.activation(sq_t[:, 0, 0:LAT], one(x3, m), ACT.Square).then_inc(sq_done, 1)

            with act.Fori(0, KT - 1) as m:
                hi("out1", 2, 2 * m + SLOT_OUT1 + 2, m, 2)
                hi("out1", 3, 2 * m + SLOT_OUT1 + 3, m, 2)
                x2_sq(m)
            for m in range(POOL_TILES):
                act.activation(tmp_t[:, m, 0:LAT], x3[:, m, :], ACT.Copy,
                               scale=g_final[:, m:m + 1]).then_inc(gained, 1)
            x2_sq(KT - 1)
            act.wait_ge(sum_sq_done, KT + 2)
            act.activation(rstd_t[:, 0:LAT], bank(4), ACT.Sqrt, scale=1.0 / D,
                           bias=eps[:, :]).then_inc(root_done, 1)

        @block.vector
        def _(dve):
            steps = [0]

            def link(instruction):
                steps[0] += 1
                instruction.then_inc(step, 1)
                dve.wait_ge(step, steps[0])

            def lo(t, n):
                dve.wait_ge(hi_done, t + 1)
                dve.tensor_tensor(ring[:, n[1], 1, :], raw[:, n[0], :], f32(ring[:, n[1], 0, :]),
                                  ALU.subtract).then_inc(split_done, 1)

            def lo_at(phase, n, t):
                lo(t, (raw_at(phase, n)[0], n % 2))

            def h_low(layer, k):
                dve.wait_ge(hhi_done, KT * layer + k + 1)
                dve.tensor_tensor(h_lo[:, k, :], tmp_t[:, k, :], f32(h_hi[:, k, :]),
                                  ALU.subtract).then_inc(hlo_done, 1)

            def decay():
                d = [dk[:, i, :] for i in range(10)]
                tt = lambda o, a, b, op: link(dve.tensor_tensor(o, a, b, op))
                ts = lambda o, a, s1, s2, op0, op1: link(dve.tensor_scalar(o, a, s1, s2, op0, op1))
                ts(d[0], d[0], -126.0, 0.0, ALU.max, ALU.add)
                link(dve.tensor_copy(dki[:, :], d[0]))
                link(dve.tensor_copy(d[1], dki[:, :]))
                tt(d[2], d[0], d[1], ALU.subtract)
                ts(d[1], d[1], 127.0, 8388608.0, ALU.add, ALU.mult)
                link(dve.tensor_copy(dki[:, :], d[1]))
                ln2 = float(np.log(2.0))
                coef = [1.0]
                for i in range(1, 10):
                    coef.append(coef[-1] * ln2 / i)
                ts(d[3], d[2], coef[9], coef[8], ALU.mult, ALU.add)
                for i in range(7, -1, -1):
                    tt(d[3], d[3], d[2], ALU.mult)
                    ts(d[3], d[3], 1.0, coef[i], ALU.mult, ALU.add)
                tt(d[3], d[3], dki[:, :].bitcast(F32), ALU.mult)
                ts(d[4], d[3], -1.0, 2.0, ALU.mult, ALU.add)
                link(dve.reciprocal(d[4], d[4]))
                tt(d[4], d[4], d[3], ALU.mult)
                tt(d[5], d[4], d[4], ALU.mult)
                ts(d[6], d[5], 1.0 / 13, 1.0 / 11, ALU.mult, ALU.add)
                for i in (9, 7, 5, 3, 1):
                    tt(d[6], d[6], d[5], ALU.mult)
                    ts(d[6], d[6], 1.0, 1.0 / i, ALU.mult, ALU.add)
                tt(d[6], d[6], d[4], ALU.mult)
                ts(d[6], d[6], -2.0, 0.0, ALU.mult, ALU.add)
                dve.tensor_scalar(d[7], d[3], -1.0, 1.0, ALU.mult, ALU.add).then_inc(rest_done, 1)
                dve.wait_ge(ln_done, 1)
                ts(d[5], d[3], 0.25, 0.0, ALU.is_gt, ALU.add)
                tt(d[7], d[7], d[6], ALU.subtract)
                tt(d[7], d[7], d[5], ALU.mult)
                tt(log_g, d[7], d[6], ALU.add)
                ts(dk[:, 8, :], log_g, -1.0, 0.0, ALU.mult, ALU.add)

            dve.sem_inc(split_done, SPLIT0)
            dve.sem_inc(rows_done, 1)
            dve.sem_inc(ds_done, 4)
            dve.sem_inc(ablo, 1)
            dve.sem_inc(x1_done, 4)
            dve.memset(eps[:, :], EPS).then_inc(eps_set, 1)
            dve.wait_ge(csf_done, 1)
            for v in range(2):
                c = csf[:, KT * v:KT * v + KT]
                link(dve.tensor_copy(cond[:, :, 2 * v], c))
                dve.tensor_tensor(cond[:, :, 2 * v + 1], c, f32(cond[:, :, 2 * v]),
                                  ALU.subtract).then_inc(cond_done, 1)
            dve.wait_ge(s_decay, 16)
            decay()
            dve.wait_ge(root_done, 1)
            dve.reciprocal(rstd_t, rstd_t).then_inc(rstd_done, 1)
            for k in range(KT):
                dve.wait_ge(ada_hi, k + 1)
                dve.tensor_tensor(ada_split[:, k % 3, 1, :], ada_raw[:, k % 4, :],
                                  f32(ada_split[:, k % 3, 0, :]), ALU.subtract).then_inc(ada_lo, 1)
            dve.wait_ge(ada_mm, KT)
            for n in range(4):
                dve.tensor_copy(rows0[:, 512 * n:512 * n + 512],
                                bank(n, parts=4)).then_inc(rows0_done, 1)
            lo_at("gate", 0, 0)
            dve.wait_ge(mod0_tr, 1)
            link(dve.tensor_copy(mod_t[:, 0:16, :], bank(6, 64).rearrange("p (t r) -> p t r", t=16)))

            def columns(mod, n, bias):
                link(dve.tensor_tensor(mod, mod_t[:, 0:n, 0:4:2], mod_t[:, 0:n, 1:4:2], ALU.add))
                link(dve.tensor_tensor(mod, mod, bias.unsqueeze(2).to_broadcast([P, n, 2]), ALU.add))

            def multiplier(layer, scale):
                g = g_norm[layer].unsqueeze(2).to_broadcast([P, KT, 2])
                link(dve.tensor_scalar(scale, scale, 1.0, 0.0, ALU.add, ALU.add))
                dve.tensor_tensor(amul[:, layer, :, :], scale, g, ALU.mult).then_inc(mods, 1)

            columns(mod0[:, :, :], 16, bias0[:, 0:16])
            multiplier(0, mod0[:, 8:16, :])
            for k in range(KT):
                h_low(0, k)
            with dve.Fori(0, Z_ITERS) as j:
                for s in range(Z_PER):
                    lo_at("gate", s + 1, Z_PER * j + s + 1)
                dve.wait_ge(slot_done, Z_PER * j + (Z_PER + DONE0))
                dve.tensor_copy(one(rows1.rearrange("p (j n) -> p j n", j=Z_ITERS), j),
                                bank(7, parts=4)).then_inc(rows_done, 1)

            def u_lo(g, tile):
                dve.wait_ge(uhi, 2 * g + tile + 1)
                dve.tensor_tensor(u[1][:, tile, :], banks[:, 1024 * tile:1024 * tile + TOK],
                                  f32(u[0][:, tile, :]), ALU.subtract).then_inc(ulo, 1)

            def ab_lo(p):
                for t in range(TT):
                    dve.wait_ge(abhi, 6 * p + t + 1)
                    dve.tensor_tensor(ab[1][:, t, :], bank(4 + t % 2, AB), f32(ab[0][:, t, :]),
                                      ALU.subtract).then_inc(ablo, 1)

            def sum_diff(p):
                dve.wait_ge(q_copied, 2 * p + 1)
                dve.wait_ge(gated, 6 * p + 4)
                for dst, op in ((d_lat, ALU.subtract), (s_lat, ALU.add)):
                    dve.tensor_tensor(dst[:, 0:HALF], bank(6, HALF), q_lat[:, 0:HALF],
                                      op).then_inc(ds_done, 1)
                dve.wait_ge(q_copied, 2 * p + 2)
                dve.wait_ge(gated, 6 * p + 6)
                for dst, op in ((d_ctx, ALU.subtract), (s_ctx, ALU.add)):
                    dve.tensor_tensor(dst, bank(4, CTX), q_ctx, op).then_inc(ds_done, 1)

            lo_at("fnet", 1, SLOT_U + 1)
            u_lo(0, 0)
            dve.wait_ge(mod1_tr, 1)
            link(dve.tensor_copy(mod_t[:, :, :], bank(4, P).rearrange("p (t r) -> p t r", t=32)))
            link(dve.memset(q_lat[:, LAT // 2:HALF], 0.0))
            link(dve.tensor_tensor(mod1[:, :, :], mod_t[:, :, 0:4:2], mod_t[:, :, 1:4:2], ALU.add))
            for a, b, bias in ((0, KT, bias0[:, 16:24]), (KT, 4 * KT, bias1)):
                link(dve.tensor_tensor(mod1[:, a:b, :], mod1[:, a:b, :],
                                       bias.unsqueeze(2).to_broadcast([P, b - a, 2]), ALU.add))
            multiplier(1, mod1[:, 2 * KT:3 * KT, :])
            lo_at("fnet", 2, SLOT_U + 2)
            u_lo(0, 1)
            with dve.Fori(1, GROUPS) as g:
                lo_at("fnet", 1, 2 * g + SLOT_U + 1)
                ab_lo(g - 1)
                u_lo(g, 0)
                lo_at("fnet", 2, 2 * g + SLOT_U + 2)
                u_lo(g, 1)
                sum_diff(g - 1)

            def g_lo(kk):
                dve.wait_ge(ghi, kk + 1)
                dve.tensor_tensor(g0(kk, 1), gate0[:, kk, :], f32(g0(kk, 0)),
                                  ALU.subtract).then_inc(glo, 1)

            lo_at("fnet", 1, SLOT_OUT0 + 1)
            ab_lo(GROUPS - 1)
            for kk in range(4):
                g_lo(kk)
            sum_diff(GROUPS - 1)
            dve.wait_ge(nyq_mm, 1)
            dve.wait_ge(s_nyqg, 16)
            dve.tensor_copy(nyq_y[:, 0:HALF], bank(5, HALF, parts=GROUPS)).then_inc(nyq_vec, 1)
            dve.tensor_copy(nyq_y[:, HALF:LAT],
                            bank(5, HALF, parts=GROUPS)[:, LAT // 2 - 1:0:-1]).then_inc(nyq_vec, 1)
            dve.tensor_copy(nyq_y[:, LAT:TOK], bank(3, CTX, parts=GROUPS)).then_inc(nyq_vec, 1)
            dve.wait_ge(nyq_vec, 3)
            dve.tensor_tensor(nyq_y, nyq_y, nyq_gate, ALU.mult).then_inc(nyq_vec, 1)
            for kk in range(4, FT):
                g_lo(kk)
            dve.wait_ge(glo, FT)
            dve.memset(acc_t, 0.0).then_inc(acc_done, 1)
            dve.wait_ge(s_xl2, 16)
            dve.wait_ge(s_xc2, 16)
            with dve.Fori(0, KT // 2) as j:
                for half in range(2):
                    m = 2 * j + half
                    lo_at("fnet", 0, 4 * j + (2 * half + SLOT_OUT0 + 2))
                    lo_at("fnet", 1, 4 * j + (2 * half + SLOT_OUT0 + 3))
                    dve.wait_ge(slot_done, 4 * j + (2 * half + SLOT_OUT0 + 2 + DONE0))
                    dve.scalar_tensor_tensor(out=one(x3, m), in0=bank(2 * half, LAT),
                                             scalar=one(mod1, m)[:, 0:1], in1=one(x3, m),
                                             op0=ALU.mult, op1=ALU.add).then_inc(x1_done, 1)
                    dve.scalar_tensor_tensor(out=one(xc3, m), in0=bank(2 * half + 1, CTX),
                                             scalar=one(mod1, m)[:, 1:2], in1=one(xc3, m),
                                             op0=ALU.mult, op1=ALU.add).then_inc(x1_done, 1)
                    dve.wait_ge(sq_done, 4 * j + (2 * half + 2 * KT + 2))
                    dve.wait_ge(acc_done, m + 1)
                    dve.tensor_tensor(acc_t, acc_t, sq_t[:, 0, :], ALU.add).then_inc(acc_done, 1)
            dve.wait_ge(root_done, 2)
            dve.reciprocal(rstd_t, rstd_t).then_inc(rstd_done, 1)
            dve.wait_ge(rstd_done, 2)

            def h_norm(k):
                dve.tensor_tensor(tmp_t[:, k, 0:LAT], x3[:, k, :], rstd_t[:, 0:LAT],
                                  ALU.mult).then_inc(t_vec, 1)
                dve.tensor_tensor(tmp_t[:, k, LAT:TOK], xc3[:, k, :], rstd_t[:, LAT:TOK],
                                  ALU.mult).then_inc(t_vec, 1)

            h_norm(0)
            h_norm(1)
            for k in range(KT):
                if k + 2 < KT and k + 2 not in (2, 5):
                    h_norm(k + 2)
                h_low(1, k)

            def o_norm(h):
                dve.wait_ge(oroot, h + 1)
                dve.reciprocal(head_rstd, head_rstd).then_inc(orstd, 1)
                dve.wait_ge(orstd, h + 1)
                for i in range(4):
                    if i >= 2:
                        dve.wait_ge(ogated, 4 * h + i - 1)
                    dve.tensor_tensor(p_f[:, i % 2, :], bank(2 + i), head_rstd,
                                      ALU.mult).then_inc(onorm, 1)

            def g1_lo(kk):
                dve.wait_ge(ghi, FT + kk + 1)
                dve.tensor_tensor(g1(kk, 1), gate1[:, kk, :], f32(g1(kk, 0)),
                                  ALU.subtract).then_inc(glo, 1)

            def head(h, first=False, last=False):
                lf, nlb = dk[:, 9, bass.ds(h, 1)], dk[:, 8, bass.ds(h + 4, 1)]

                def used(s):
                    lo_at("head", s + 2, HEAD_PER * h + (SLOT_HEAD + s + 2))

                def turns(n, a, b):
                    for dst, src, w in ((0, a, cos_t), (1, b, sin_t), (2, a, sin_t), (3, b, cos_t)):
                        dve.tensor_tensor(turn[dst], bank(src), w, ALU.mult).then_inc(turned, 1)

                def part_lo(n, dst, src):
                    dve.wait_ge(qkhi, 6 * h + n)
                    dve.tensor_tensor(dst[1], src, f32(dst[0]), ALU.subtract).then_inc(qklo, 1)

                def both(t, i, a, b):
                    return t[0][:, i, a:b], t[1][:, i, a:b]

                used(0)
                used(1)
                turns(0, 0, 1)
                part_lo(1, both(q_s, 0, 0, LAT), turn[0])
                part_lo(2, both(q_s, 1, 0, LAT), turn[2])
                used(2)
                if not first:
                    o_norm(h - 1)
                used(3)
                used(4)
                part_lo(3, both(k_s, 0, LAT, TOK), bank(3, CTX))
                used(5)
                dve.wait_ge(qklo, 6 * h + 2)
                turns(1, 2, 4)
                part_lo(4, both(k_s, 1, LAT, TOK), bank(5, CTX))
                part_lo(5, both(k_s, 0, 0, LAT), turn[0])
                part_lo(6, both(k_s, 1, 0, LAT), turn[2])
                used(6)
                dve.wait_ge(qklo, 6 * h + 6)
                dve.tensor_scalar(strip_ctx, dist[:, 0:640], float(LAT), lf, ALU.add,
                                  ALU.mult).then_inc(expo_done, 1)
                dve.tensor_scalar(dexp[:, 0:640], dist[:, 0:640], float(LAT - TOK), nlb, ALU.add,
                                  ALU.mult).then_inc(expo_done, 1)
                used(7)
                dve.wait_ge(exp_done, 3 * h + 2)
                dve.tensor_tensor(strip_ctx, strip_ctx, dexp[:, 0:640],
                                  ALU.add).then_inc(strip_done, 1)
                dve.wait_ge(strip_done, 2 * h + 1)
                dve.tensor_scalar(dexp, dist[:, :], 0.0, nlb, ALU.min, ALU.mult).then_inc(expo_done, 1)
                dve.tensor_scalar(strip_lat, dist[:, :], 0.0, lf, ALU.max, ALU.mult).then_inc(expo_done, 1)
                dve.wait_ge(expo_done, 5 * h + 4)
                dve.tensor_tensor(strip_lat, strip_lat, dexp, ALU.add).then_inc(expo_done, 1)
                used(8)
                dve.wait_ge(exp_done, 3 * h + 3)
                dve.scalar_tensor_tensor(out=strip_lat, in0=dist[:, :], scalar=0.0, in1=strip_lat,
                                         op0=ALU.is_equal, op1=ALU.add).then_inc(strip_done, 1)
                used(9)
                used(10)
                for t in range(TT):
                    dve.wait_ge(vhi, 6 * h + t + 1)
                    dve.tensor_tensor(v_s[1][:, t, :], bank(V_BANK[t]), f32(v_s[0][:, t, :]),
                                      ALU.subtract).then_inc(vlo, 1)
                used(11)
                dve.wait_ge(strip_done, 2 * h + 2)

                def decayed(t):
                    strip = (strip_lat[:, 384 - P * t:384 - P * t + LAT] if t < 4 else
                             strip_ctx[:, P * (5 - t):P * (5 - t) + LAT])
                    dve.wait_ge(score_done, 6 * h + t + 1)
                    if t >= 2:
                        dve.wait_ge(plo, 6 * h + t - 1)
                    dve.scalar_tensor_tensor(out=p_f[:, t % 2, :], in0=bank(6 + t % 2),
                                             scalar=QK ** -0.5, in1=strip, op0=ALU.mult,
                                             op1=ALU.mult).then_inc(pf_done, 1)

                if not first:
                    dve.wait_ge(ogated, 4 * h)
                decayed(0)
                for t in range(TT):
                    if t + 1 < TT:
                        decayed(t + 1)
                    dve.wait_ge(phi, 6 * h + t + 1)
                    dve.tensor_tensor(p_s[1][:, t % 2, :], p_f[:, t % 2, :], f32(p_s[0][:, t % 2, :]),
                                      ALU.subtract).then_inc(plo, 1)
                    if last:
                        g1_lo(2 * t)
                        g1_lo(2 * t + 1)

            dve.wait_ge(s_rope, 16)
            dve.wait_ge(dist_set, 1)
            head(0, first=True)
            with dve.Fori(1, HEADS - 1) as h:
                head(h)
            head(HEADS - 1, last=True)
            o_norm(HEADS - 1)
            for kk in range(12, FT):
                g1_lo(kk)
            dve.wait_ge(ogated, FT)
            dve.memset(acc_t[:, 0:LAT], 0.0).then_inc(acc_done, 1)

            def residual(m, b, n):
                if n is not None:
                    lo_at("out1", 2, n)
                    lo_at("out1", 3, n + 1)
                dve.wait_ge(slot_done, 2 * m + (SLOT_OUT1 + 2 + DONE0))
                dve.scalar_tensor_tensor(out=one(x3, m), in0=bank(b), scalar=one(mod1, m + 24)[:, 0:1],
                                         in1=one(x3, m), op0=ALU.mult,
                                         op1=ALU.add).then_inc(x1_done, 1)
                dve.wait_ge(sq_done, m + (4 * KT + 1))
                dve.wait_ge(acc_done, m + (KT + 2))
                dve.tensor_tensor(acc_t[:, 0:LAT], acc_t[:, 0:LAT], sq_t[:, 0, 0:LAT],
                                  ALU.add).then_inc(acc_done, 1)

            residual(0, 0, SLOT_OUT1 + 2)
            with dve.Fori(0, 3) as j:
                residual(2 * j + 1, 1, 4 * j + (SLOT_OUT1 + 4))
                residual(2 * j + 2, 0, 4 * j + (SLOT_OUT1 + 6))
            residual(7, 1, None)
            dve.wait_ge(root_done, 3)
            dve.reciprocal(rstd_t[:, 0:LAT], rstd_t[:, 0:LAT]).then_inc(rstd_done, 1)
            dve.wait_ge(rstd_done, 3)
            for m in range(POOL_TILES, KT):
                dve.scalar_tensor_tensor(out=x3[:, m, :], in0=x3[:, m, :], scalar=g_final[:, m:m + 1],
                                         in1=rstd_t[:, 0:LAT], op0=ALU.mult,
                                         op1=ALU.mult).then_inc(out_vec, 1)

        @block.tensor
        def _(pe):
            def mm3(out, left, right, start, stop):
                pe.matmul(out, left[0], right[0], start=start, stop=False)
                pe.matmul(out, left[0], right[1], start=False, stop=False)
                return pe.matmul(out, left[1], right[0], start=False, stop=stop)

            def split(t):
                pe.wait_ge(split_done, t + (1 + SPLIT0))

            def slot_tile(par, k):
                return ring[:, par, 0, P * k:P * k + P], ring[:, par, 1, P * k:P * k + P]

            def h_part(k, a, b):
                return h_hi[:, k, a:b], h_lo[:, k, a:b]

            def project(par, chunks, ready=None):
                for k in range(KT):
                    if ready is not None:
                        pe.wait_ge(hlo_done, ready + k + 1)
                    for a, b, o in chunks:
                        last = mm3(o, slot_tile(par, k), h_part(k, a, b), k == 0, k == KT - 1)
                last.then_inc(slot_done, 1)

            def both_chunks(b):
                return (0, LAT, bank(b)), (LAT, TOK, bank(b + 1, CTX))

            pe.sem_inc(slot_done, DONE0)
            pe.wait_ge(ones_set, 1)
            for k in range(KT):
                pe.wait_ge(sq_done, 2 * k + 2)
                pe.matmul(bank(4), ones[:, :], sq_t[:, k % 2, 0:LAT], start=k == 0, stop=k == KT - 1)
                pe.matmul(bank(5, CTX), ones[:, :], sq_t[:, k % 2, LAT:TOK], start=k == 0,
                          stop=k == KT - 1).then_inc(sum_sq_done, 1)
            pe.wait_ge(cond_done, 2)
            for k in range(KT):
                pe.wait_ge(ada_lo, k + 1)
                for n in range(4):
                    for part in range(2):
                        last = pe.matmul(bank(n, parts=4), cond[:, k, :],
                                         ada_split[:, k % 3, part, 512 * n:512 * n + 512],
                                         start=k == 0 and part == 0, stop=k == KT - 1 and part == 1)
                last.then_inc(ada_mm, 1)
            pe.wait_ge(rows0_done, 4)
            pe.wait_ge(ident_set, 2)
            for i in range(16):
                last = pe.transpose(bank(6, 4, 4 * i), rows0[:, P * i:P * i + P], ident4[:, :])
            last.then_inc(mod0_tr, 1)

            with pe.Fori(0, Z_ITERS) as j:
                for s in range(Z_PER):
                    split(Z_PER * j + s)
                    if s % 3 == 0:
                        pe.wait_ge(z_done, 2 * j + (s // 3 + 1))
                        project(s % 2, both_chunks(2 * (s // 3)), 0 if s == 0 else None)
                        continue
                    quarter = (1, 2, 4, 5).index(s)
                    if quarter == 0:
                        pe.wait_ge(rows_done, j + 1)
                    for i in range(2):
                        for part in range(2):
                            last = pe.matmul(bank(7, parts=4), cond[:, 2 * quarter + i, :],
                                             ring[:, s % 2, part, 512 * i:512 * i + 512],
                                             start=quarter == 0 and i == 0 and part == 0,
                                             stop=quarter == 3 and i == 1 and part == 1)
                    last.then_inc(slot_done, 1)

            def u_tile(g, tile):
                split(2 * g + (SLOT_U + tile))
                project(tile, both_chunks(2 * tile))

            def features(p):
                pe.wait_ge(ulo, 2 * p + 2)
                for t in range(TT):
                    if t == 0:
                        pe.wait_ge(ds_done, 4 * p + 4)
                    else:
                        pe.wait_ge(ablo, 6 * p + t)
                    for k in range(2):
                        last = mm3(bank(4 + t % 2, AB),
                                   (u[0][:, k, P * t:P * t + P], u[1][:, k, P * t:P * t + P]),
                                   (feat[0][:, k, :], feat[1][:, k, :]), k == 0, k == 1)
                    last.then_inc(feat_done, 1)

            def tokens(p):
                pe.wait_ge(ablo, 6 * p + (TT + 1))
                pe.wait_ge(ds_done, 4 * p + 2)

                def product(out, col, table, t0, n):
                    for t in range(n):
                        last = mm3(out, (ab[0][:, t0 + t, col:col + P], ab[1][:, t0 + t, col:col + P]),
                                   (table[0][:, t, :], table[1][:, t, :]), t == 0, t == n - 1)
                    return last

                product(bank(6, NB), 0, lat_cos, 0, 4)
                product(bank(7, LAT // 2), P, lat_sin, 0, 4).then_inc(seq_done, 1)
                product(bank(4, CTX), 0, ctx_cos, 4, 2)
                product(bank(4, CTX, CTX), P, ctx_sin, 4, 2).then_inc(seq_done, 1)

            pe.wait_ge(z_done, FT + 1)
            u_tile(0, 0)
            pe.wait_ge(rows_done, Z_ITERS + 1)
            for i in range(32):
                last = pe.transpose(bank(4, 4, 4 * i), rows1[:, P * i:P * i + P], ident4[:, :])
            last.then_inc(mod1_tr, 1)
            pe.wait_ge(z_done, FT + 2)
            u_tile(0, 1)
            pe.wait_ge(s_tables, 16)
            with pe.Fori(1, GROUPS) as g:
                pe.wait_ge(ulo, 2 * g - 1)
                u_tile(g, 0)
                features(g - 1)
                pe.wait_ge(ulo, 2 * g)
                u_tile(g, 1)
                tokens(g - 1)
            features(GROUPS - 1)
            tokens(GROUPS - 1)
            pe.wait_ge(nyq_copied, 2 * GROUPS + 2)
            for t in range(4):
                mm3(bank(5, NB, parts=GROUPS), (nyq[0][:, t, :], nyq[1][:, t, :]),
                    (lat_cos[0][:, t, :], lat_cos[1][:, t, :]), t == 0, t == 3)
            for t in range(2):
                last = mm3(bank(3, CTX, parts=GROUPS), (nyq[0][:, 4 + t, :], nyq[1][:, 4 + t, :]),
                           (ctx_cos[0][:, t, :], ctx_cos[1][:, t, :]), t == 0, t == 1)
            last.then_inc(nyq_mm, 1)

            def out_tile(t, chunks, g, ready):
                for half in range(2):
                    split(t + half)
                    for k in range(8):
                        kk = 8 * half + k
                        pe.wait_ge(glo, ready + kk + 1)
                        for a, b, o in chunks:
                            last = mm3(o, slot_tile(half, k), (g(kk, 0)[:, a:b], g(kk, 1)[:, a:b]),
                                       kk == 0, kk == FT - 1)
                    last.then_inc(slot_done, 1)
                    yield

            with pe.Fori(0, KT // 2) as j:
                for half in range(2):
                    pe.wait_ge(x1_done, 4 * j + (2 * half + 2))
                    if half:
                        pe.wait_ge(nyq_vec, 3)
                    for _ in out_tile(4 * j + (2 * half + SLOT_OUT0), both_chunks(2 * half), g0, 0):
                        pass
            pe.wait_ge(acc_done, KT + 1)
            pe.matmul(bank(4), ones[:, :], acc_t[:, 0:LAT], start=True, stop=True)
            pe.matmul(bank(5, CTX), ones[:, :], acc_t[:, LAT:TOK], start=True,
                      stop=True).then_inc(sum_sq_done, 1)

            def o_sum(h):
                pe.wait_ge(oacc, 3 * h + 3)
                pe.matmul(bank(6), ones[:, :], head_rstd, start=True, stop=True).then_inc(oss, 1)

            def head(h, first=False):
                def lat(s, b, ready=None):
                    split(HEAD_PER * h + (SLOT_HEAD + s))
                    project(s % 2, ((0, LAT, bank(b)),), ready)

                def all_tokens(s, b):
                    split(HEAD_PER * h + (SLOT_HEAD + s))
                    project(s % 2, both_chunks(b))

                if not first:
                    pe.wait_ge(vlo, 6 * h)
                lat(0, 0, KT if first else None)
                lat(1, 1)
                if not first:
                    pe.wait_ge(pf_done, 6 * h)
                    o_sum(h - 1)
                lat(2, 7)
                if not first:
                    pe.wait_ge(oroot, h)
                lat(3, 6)
                if not first:
                    pe.wait_ge(onorm, 4 * h)
                all_tokens(4, 2)
                all_tokens(5, 4)
                pe.wait_ge(z1_done, 4 * h + 1)
                lat(6, 7)
                pe.wait_ge(turned, 8 * h + 8)
                pe.wait_ge(qklo, 6 * h + 4)
                for s in range(7, 11):
                    split(HEAD_PER * h + (SLOT_HEAD + s))
                    for i in range(2):
                        k = 2 * (s - 7) + i
                        w = tuple(ring[:, s % 2, part, DV * i:DV * i + DV] for part in range(2))
                        for t in range(TT):
                            last = mm3(bank(V_BANK[t]), h_part(k, P * t, P * t + P), w, k == 0,
                                       k == KT - 1)
                    last.then_inc(slot_done, 1)
                pe.wait_ge(z1_done, 4 * h + 3)
                lat(11, 7)

                def scores(t):
                    if t < 2:
                        pe.wait_ge(z1_done, 4 * h + 2 * t + 2)
                    else:
                        pe.wait_ge(pf_done, 6 * h + t - 1)
                    for i in range(2):
                        last = mm3(bank(6 + t % 2),
                                   (k_s[0][:, i, P * t:P * t + P], k_s[1][:, i, P * t:P * t + P]),
                                   (q_s[0][:, i, :], q_s[1][:, i, :]), i == 0, i == 1)
                    last.then_inc(score_done, 1)

                pe.wait_ge(qklo, 6 * h + 6)
                scores(0)
                scores(1)
                for t in range(TT):
                    if t == 0:
                        pe.wait_ge(vlo, 6 * h + 4)
                    else:
                        pe.wait_ge(vlo, 6 * h + t + 1)
                    pe.wait_ge(plo, 6 * h + t + 1)
                    for i in range(4):
                        last = mm3(bank(2 + i),
                                   (v_s[0][:, t, P * i:P * i + P], v_s[1][:, t, P * i:P * i + P]),
                                   (p_s[0][:, t % 2, :], p_s[1][:, t % 2, :]), t == 0, t == TT - 1)
                    last.then_inc(pv_done, 1)
                    if t + 2 < TT:
                        scores(t + 2)

            head(0, first=True)
            with pe.Fori(1, HEADS) as h:
                head(h)

            def last_tile(m, b):
                pe.wait_ge(x1_done, m + (2 * KT - 1 + 4))
                return out_tile(2 * m + SLOT_OUT1, ((0, LAT, bank(b)),), g1, FT)

            pe.wait_ge(vlo, 6 * HEADS)
            for n, _ in enumerate(last_tile(0, 0)):
                if n == 0:
                    o_sum(HEADS - 1)
            with pe.Fori(0, 3) as j:
                for _ in last_tile(2 * j + 1, 1):
                    pass
                for _ in last_tile(2 * j + 2, 0):
                    pass
            for _ in last_tile(7, 1):
                pass
            pe.wait_ge(acc_done, 2 * KT + 2)
            pe.matmul(bank(4), ones[:, :], acc_t[:, 0:LAT], start=True, stop=True).then_inc(sum_sq_done, 1)


def mtile(w, cols):
    return w[:, cols].reshape(KT, P, P).transpose(1, 0, 2).reshape(P, SLOT)


def wide(w, first, k):
    return w[2 * P * k:2 * P * (k + 1), first:first + 512].reshape(2, P, 512).transpose(
        1, 0, 2).reshape(P, SLOT)


def weight_stream(ada_w, fnet_in, fnet_out, ret_in, ret_out):
    i = np.arange(P)
    low = [GDIM * g + i for g in range(GROUPS)]
    high = [GDIM * g + np.where(i == 0, P, GDIM - i) for g in range(GROUPS)]
    feats = low + high
    slots = []
    for j in range(Z_ITERS):
        layer, first = (0, 2 * D + 512 * j) if j < 2 else (1, 512 * (j - 2))
        ada = [wide(ada_w[layer], first, k) for k in range(4)]
        for half in range(2):
            slots += [mtile(fnet_in, DB + feats[2 * j + half])] + ada[2 * half:2 * half + 2]
    for n in range(2 * GROUPS):
        slots.append(mtile(fnet_in, P * n + i))
    order = np.concatenate(feats)
    for m in range(KT):
        for half in range(2):
            slots.append(mtile(fnet_out[order[D * half:D * half + D]], P * m + i))
    quarter = QK // 4
    x1 = np.concatenate([np.arange(quarter), 2 * quarter + np.arange(quarter)])
    for h in range(HEADS):
        q = [mtile(ret_in, QK * h + x1 + quarter * n) for n in range(2)]
        k = [mtile(ret_in, D + QK * h + x1 + quarter * n) for n in range(2)]
        v = [wide(ret_in, 2 * D + DV * h, n) for n in range(4)]
        z = [mtile(ret_in, 2 * D + DB + DV * h + P * n + i) for n in range(4)]
        slots += q + z[0:2] + k + z[2:3] + v + z[3:4]
    for m in range(KT):
        for half in range(2):
            slots.append(mtile(ret_out[D * half:D * half + D], P * m + i))
    assert len(slots) == SLOTS
    return np.stack(slots)


def columns(v):
    return v.reshape(-1, P).T


def kernel(x, c, ctx, c_ctx, norm_g, ada_w, ada_b, fnet_w_in, fnet_w_out, ret_w_in, ret_w_out,
           ret_decay, final_g):
    import concourse.bacc as bacc
    from concourse.bass_utils import run_bass_kernel_spmd

    (x, c, ctx, c_ctx, norm_g, ada_w, ada_b, fnet_w_in, fnet_w_out, ret_w_in, ret_w_out, ret_decay,
     final_g) = (np.asarray(a) for a in (x, c, ctx, c_ctx, norm_g, ada_w, ada_b, fnet_w_in,
                                         fnet_w_out, ret_w_in, ret_w_out, ret_decay, final_g))

    def transposed(a):
        return a.T.reshape(KT, P, -1).transpose(1, 0, 2).reshape(P, -1)

    arrays = {
        "x_lat": transposed(x[0]),
        "x_ctx": transposed(ctx[0]),
        "small_in": np.concatenate([columns(c[0]), columns(c_ctx), columns(norm_g[0]),
                                    columns(norm_g[1]), columns(final_g), columns(ada_b[0]),
                                    columns(ada_b[1])], 1),
        "decay_in": ret_decay[0].reshape(8),
        "ada_first": ada_w[0].reshape(KT, P, 3 * D)[:, :, 0:2 * D],
        "stream": weight_stream(ada_w, fnet_w_in[0], fnet_w_out[0], ret_w_in[0], ret_w_out[0]),
        "tables_in": dft_tables(),
        "rope_in": rope_tables(),
    }
    arrays = {n: np.ascontiguousarray(a) for n, a in arrays.items()}
    nc = bacc.Bacc("TRN2", target_bir_lowering=False, num_devices=1)
    args = [nc.dram_tensor(n, a.shape, F32, kind="ExternalInput").ap() for n, a in arrays.items()]
    out = nc.dram_tensor("out", (KT, P, LAT), F32, kind="ExternalOutput").ap()
    build(nc, *args, out)
    result = run_bass_kernel_spmd(nc, [arrays], core_ids=[0]).results[0]["out"]
    return result.reshape(D, LAT).T.reshape(1, LAT, D)
```

```python
from contextlib import ExitStack

import numpy as np

import concourse.bass as bass
from concourse import mybir

F32 = mybir.dt.float32
F32R = mybir.dt.float32r
I32 = mybir.dt.int32
ALU = mybir.AluOpType
ACT = mybir.ActivationFunctionType

P = 128
D = 1024
KT = D // P
LAT, CTX = 512, 256
TOK = LAT + CTX
TT = TOK // P
DB = 2048
FT = DB // P
GROUPS, GDIM = 8, 256
HEADS, QK, DV = 4, 256, 512
GRID_W = 64
ROPE_BASE = 10000.0
EPS = 1e-6
HALF = LAT // 2 + 1
CHALF = CTX // 2 + 1
NF = HALF + CHALF
NB = HALF + 1
WCOLS = GDIM + 2
SLOT = 1024

SLOT_ADA0 = 2
SLOT_U = SLOT_ADA0 + 16
SLOT_Z = SLOT_U + 2 * (GROUPS - 1)
Z_PER = 6
SLOT_OUT0 = SLOT_Z + Z_PER * GROUPS
SLOT_HEAD = SLOT_OUT0 + 2 * KT
HEAD_PER = 12
SLOT_OUT1 = SLOT_HEAD + HEAD_PER * HEADS
SLOTS = SLOT_OUT1 + 2 * KT
RAW_BUFS = 3
CHUNKS = 4 + GROUPS
V_BANK = (0, 2, 3, 4, 5, 1)
POOL_TILES = 3
DONE0 = 4
SPLIT0 = 6

PHASES = {
    "start": (0, 3, 0, (0, 0, 0)),
    "u": (SLOT_U, 2, 0, (6, 6, 6)),
    "z": (SLOT_Z, 3, 2, (13, 13, 6)),
    "out0": (SLOT_OUT0, 2, 0, (29, 29, 22)),
    "head": (SLOT_HEAD, 3, 2, (37, 37, 22)),
    "out1": (SLOT_OUT1, 2, 0, (53, 53, 38)),
}


def raw_at(phase, n):
    _, bufs, first, before = PHASES[phase]
    buf = (n + first) % bufs
    return buf, 16 * (before[buf] + n // bufs + 1)


def raw_step(phase, per_iteration):
    return 16 * (per_iteration // PHASES[phase][1])


def dft_tables():
    p = np.arange(P)[:, None, None]

    def phase(tiles, cols, n):
        rows = p + P * np.arange(tiles)[None, :, None]
        return 2 * np.pi * ((rows * np.asarray(cols)[None, None, :]) % n) / n

    k = np.arange(P)
    feat = np.concatenate([np.cos(phase(2, k, GDIM)), np.sin(phase(2, k, GDIM)),
                           np.cos(phase(2, [P], GDIM)), np.zeros((P, 2, 1))], 2) / np.sqrt(GDIM)
    lat_cos = np.cos(phase(4, np.arange(NB), LAT)) / np.sqrt(LAT)
    lat_sin = np.concatenate([np.sin(phase(4, np.arange(1, HALF - 1), LAT)),
                              np.zeros((P, 4, 1))], 2) / np.sqrt(LAT)
    ctx = np.concatenate([np.cos(phase(2, np.arange(CHALF), CTX)),
                          np.sin(phase(2, np.arange(1, CHALF - 1), CTX))], 2) / np.sqrt(CTX)
    return np.ascontiguousarray(np.concatenate(
        [t.reshape(P, -1) for t in (feat, lat_cos, lat_sin, ctx)], 1).astype(np.float32))


def rope_tables():
    nf = QK // 4
    freqs = ROPE_BASE ** (-np.arange(nf, dtype=np.float32) / np.float32(nf))
    pos = np.arange(LAT)
    ang = np.concatenate([freqs[:, None] * (pos // GRID_W)[None, :].astype(np.float32),
                          freqs[:, None] * (pos % GRID_W)[None, :].astype(np.float32)], 0)
    return np.ascontiguousarray(np.concatenate([np.cos(ang), np.sin(ang)], 1).astype(np.float32))


TRANSFORM_PARTS = ((0, 0, 1, 1, HALF - 1), (1, 0, HALF + 1, HALF + 1, CHALF - 1),
                   (0, 1, 1, NF, HALF - 2), (1, 1, HALF + 1, NF + HALF - 2, CHALF - 2))
FEAT_COLS = 2 * WCOLS
TABLE_COLS = FEAT_COLS + 4 * NB + 4 * (LAT // 2) + 2 * CTX


def build(nc, x_lat, x_ctx, x_rows, small_in, decay_in, stream, tables_in, rope_in, out):
    ctx = ExitStack()
    with ctx:
        def sb(name, shape, dt=F32):
            return ctx.enter_context(nc.sbuf_tensor(name, shape, dt))

        def sem(name):
            return ctx.enter_context(nc.semaphore(name))

        ring = sb("ring", [P, 2, 2, SLOT], F32R)
        hreg = sb("hreg", [P, 4 * KT * NF], F32R)
        WREG = 13312
        wreg = sb("wreg", [P, WREG], F32R)
        cond = sb("cond", [P, KT, 4], F32R)
        xreg = sb("xreg", [P, 2 * KT * NF])
        gate = sb("gate", [P, FT * TOK])
        raw = sb("raw", [P, RAW_BUFS, SLOT])
        small = sb("small", [P, 88])
        csf = sb("csf", [P, 2 * KT])
        mod_t = sb("mod_t", [P, 4 * CHUNKS, 4])
        mod0 = sb("mod0", [P, 16, 2])
        mod1 = sb("mod1", [P, 32, 2])
        amul = sb("amul", [P, 2, KT, 2])
        ones = sb("ones", [P, P])
        ident4 = sb("ident4", [4, 4])
        eps = sb("eps", [P, 1])
        dk = sb("dk", [P, 10, 8])
        dki = sb("dki", [P, 8], I32)
        dist = sb("dist", [P, 512 + NF])
        banks = ctx.enter_context(nc.psum_tensor("banks", [P, 8 * 512], F32))

        def bank(b, n=512, off=0, parts=P):
            return banks[0:parts, 512 * b + off:512 * b + off + n]

        def f32(ap):
            return ap.bitcast(F32)

        def one(ap, i):
            return ap[:, bass.ds(i, 1), :].rearrange("p a n -> p (a n)")

        h_hi = hreg[:, 0:KT * TOK].rearrange("p (k t) -> p k t", k=KT)
        h_lo = hreg[:, KT * TOK:2 * KT * TOK].rearrange("p (k t) -> p k t", k=KT)
        xl, xc = xreg[:, 0:KT * LAT], xreg[:, KT * LAT:KT * TOK]
        TAIL = 8192
        sq_t = gate[:, TAIL:TAIL + 2 * TOK].rearrange("p (b n) -> p b n", b=2)
        cos_t = gate[:, TAIL + 1536:TAIL + 2048]
        sin_t = gate[:, TAIL + 2048:TAIL + 2560]
        acc_t = gate[:, TAIL + 2560:TAIL + 2560 + TOK]
        rstd_t = gate[:, TAIL + 3328:TAIL + 3328 + TOK]
        tmp_t = gate[:, 0:KT * TOK].rearrange("p (k t) -> p k t", k=KT)
        gate0 = gate[:, :].rearrange("p (f t) -> p f t", f=FT)
        gate1 = gate[:, 0:FT * LAT].rearrange("p (f t) -> p f t", f=FT)
        x3 = xl.rearrange("p (k t) -> p k t", k=KT)
        xc3 = xc.rearrange("p (k t) -> p k t", k=KT)

        x_tok = gate[:, 0:TT * D].rearrange("p (t n) -> p t n", t=TT)
        xs = [hreg[:, TT * D * i:TT * D * (i + 1)].rearrange("p (t n) -> p t n", t=TT)
              for i in range(2)]
        xf = gate[:, TT * D:2 * TT * D].rearrange("p (k n) -> p k n", k=KT)
        squares = gate[:, TT * D:TT * D + 2 * D].rearrange("p (b n) -> p b n", b=2)
        hf = [[hreg[:, (2 * part + kind) * KT * NF:(2 * part + kind + 1) * KT * NF].rearrange(
            "p (k n) -> p k n", k=KT) for kind in range(2)] for part in range(2)]
        ident = gate[:, TT * D:TT * D + P]
        diag = gate[:, TT * D + P:TT * D + P + TOK].rearrange("p (t n) -> p t n", t=TT)
        rstd0 = gate[:, TT * D + P + TOK:TT * D + P + 2 * TOK]
        y3 = xreg[:, :].rearrange("p (g n) -> p g n", g=GROUPS)

        tables = [wreg[:, TABLE_COLS * i:TABLE_COLS * (i + 1)] for i in range(2)]
        at = [0]

        def take(a, b):
            v = wreg[:, at[0]:at[0] + a * b].rearrange("p (a b) -> p a b", a=a)
            at[0] += a * b
            return v

        feat, lat_cos, lat_sin, ctx_tab = [], [], [], []
        for _ in range(2):
            feat.append(take(2, WCOLS))
            lat_cos.append(take(4, NB))
            lat_sin.append(take(4, LAT // 2))
            ctx_tab.append(take(2, CTX))
        assert at[0] == 2 * TABLE_COLS
        wf = [take(KT, WCOLS), take(KT, WCOLS)]
        nyq_w = [take(KT, GROUPS), take(KT, GROUPS)]
        assert at[0] <= WREG
        rows = dist[0:4, 0:512]
        nyq_p = dist[0:GROUPS, 512:512 + NF]
        tok_ss, tok_rstd = dist[:, TOK:TOK + TT], dist[:, TOK + 8:TOK + 8 + TT]
        shift0 = dist[:, TOK + 16:TOK + 32].rearrange("p (k v) -> p k v", v=2)
        q_f = gate[:, TT * D + P + 2 * TOK:TT * D + P + 2 * TOK + NF]

        def g0(kk, part):
            r = wreg if kk < 8 else hreg
            o = (kk % 8) * 2 * TOK + part * TOK
            return r[:, o:o + TOK]

        def g0_hi_at(kk):
            return one(wreg[:, 0:8 * 2 * TOK].rearrange("p (k n) -> p k n", k=8)[:, :, 0:TOK], kk)

        def g0_lo_at(kk):
            return one(wreg[:, 0:8 * 2 * TOK].rearrange("p (k n) -> p k n", k=8)[:, :, TOK:], kk)

        def g1(kk, part):
            r = hreg if kk < 12 else wreg
            o = (kk % 12) * 2 * LAT + part * LAT
            return r[:, o:o + LAT]

        at[0] = 0
        q_s = [take(2, LAT), take(2, LAT)]
        k_s = [take(2, TOK), take(2, TOK)]
        v_s = [take(TT, DV), take(TT, DV)]
        p_s = [take(2, LAT), take(2, LAT)]
        assert at[0] <= WREG
        turn = [xc[:, 512 * i:512 * (i + 1)] for i in range(4)]
        dexp = xc[:, 0:896]
        strip_lat = gate[:, TAIL:TAIL + 896]
        strip_ctx = gate[:, TAIL + 896:TAIL + 1536]
        p_f = gate[:, TAIL + 2560:TAIL + 3584].rearrange("p (b n) -> p b n", b=2)
        head_rstd = gate[:, TAIL + 3584:TAIL + 4096]

        g_norm = [small[:, 16:24], small[:, 24:32]]
        g_final = small[:, 32:40]
        bias0, bias1 = small[:, 40:64], small[:, 64:88]
        log_g = dk[:, 9, :]

        s_small, s_decay, s_feat = sem("small_in"), sem("decay_in"), sem("feat_in")
        s_tok = sem("token_tables_in")
        s_x = [sem(f"x_tokens_in{i}") for i in range(TT)]
        s_raw = [sem(f"raw_in{i}") for i in range(RAW_BUFS)]
        s_xt, s_rope, s_out = sem("x_columns_in"), sem("rope_in"), sem("out_stored")
        s_xl2, s_xc2 = sem("xl_again"), sem("xc_again")
        s_row = sem("nyq_row_in")
        ones_set, ident4_set, ident_set = sem("ones_set"), sem("ident4_set"), sem("ident_set")
        eps_set = sem("eps_set")
        hi_done, split_done, slot_done = sem("hi_done"), sem("split_done"), sem("slot_done")
        csf_done, cond_done = sem("csf_done"), sem("cond_done")
        tab_hi, tab_lo = sem("table_hi_done"), sem("table_lo_done")
        wf_mm, wf_hi, wf_lo = sem("wf_mm_done"), sem("wf_hi_done"), sem("wf_lo_done")
        nyq_copied = sem("nyq_copied")
        tok_sq, tok_root, tok_rstd_done = sem("tok_sq_done"), sem("tok_root_done"), sem("tok_rstd")
        xs_hi, xs_hi_act, xs_lo = sem("x_hi_done"), sem("x_hi_by_scalar"), sem("x_lo_done")
        dft_done, sine_out, cosine_out = sem("dft_done"), sem("sine_out"), sem("cosine_out")
        rows_done, rows_tr, mod_copied = sem("rows_done"), sem("rows_tr"), sem("mod_copied")
        turning = sem("turning")
        mods, shift_done = sem("mods_done"), sem("shift_done")
        hf_hi, hf_lo = sem("h_transform_hi"), sem("h_transform_lo")
        diag_done, rstd_row_mm, rstd_row = sem("diag_done"), sem("rstd_row_mm"), sem("rstd_row")
        x_normed, h_made = sem("x_normed"), sem("h_made")
        hhi_done, hlo_done = sem("h_hi_done"), sem("h_lo_done")
        u_done, q_copied, ds_done = sem("u_done"), sem("q_copied"), sem("ds_done")
        nyq_mm, nyq_vec = sem("nyq_mm"), sem("nyq_vec")
        z_done, gated = sem("z_done"), sem("gated")
        ghi, glo = sem("g_hi_done"), sem("g_lo_done")
        x1_done, sq_done, acc_done = sem("x1_done"), sem("sq_done"), sem("acc_done")
        scaled, sum_sq_done = sem("x_scaled"), sem("sum_sq_done")
        root_done, rstd_done = sem("root_done"), sem("rstd_done")
        t_vec, t_pool = sem("t_vec"), sem("t_pool")
        vec_gated = sem("o_gated_by_vector")
        warm, pool_step = sem("root_table_loaded"), sem("gpsimd_step")
        step, rest_done, ln_done = sem("vector_step"), sem("rest_done"), sem("ln_done")
        turned, summed = sem("turned"), sem("turn_summed")
        qkhi, qklo = sem("qk_hi_done"), sem("qk_lo_done")
        z1_done, vhi, vlo = sem("z1_done"), sem("v_hi_done"), sem("v_lo_done")
        dist_set, expo_done, exp_done = sem("dist_set"), sem("expo_done"), sem("exp_done")
        strip_done = sem("strip_done")
        score_done, pf_done, phi, plo = (sem("score_done"), sem("p_f_done"), sem("p_hi_done"),
                                         sem("p_lo_done"))
        pv_done = sem("pv_done")
        osq, oacc, oss = sem("o_sq_done"), sem("o_acc_done"), sem("o_sum_sq_done")
        oroot, orstd, onorm, ogated = (sem("o_root_done"), sem("o_rstd_done"), sem("o_norm_done"),
                                       sem("o_gated"))
        gained, out_vec, out_pool = sem("gained"), sem("out_vec"), sem("out_pool")

        block = ctx.enter_context(nc.Block())


        @block.sync
        def _(sp):
            def load(phase, n, t):
                bufs = PHASES[phase][1]
                buf = raw_at(phase, n)[0]
                sp.wait_ge(split_done, 2 * t + (2 - 2 * bufs + SPLIT0))
                sp.dma_start(raw[:, buf, :], stream[t]).then_inc(s_raw[buf], 16)

            sp.dma_start(small[:, :], small_in).then_inc(s_small, 16)
            sp.dma_start(dk[:, 0, :], decay_in.partition_broadcast(P)).then_inc(s_decay, 16)
            sp.dma_start(xreg[:, 0:FEAT_COLS], tables_in[:, 0:FEAT_COLS]).then_inc(s_feat, 16)
            for t in range(2):
                load("start", t, t)
            for t in range(TT):
                if t == 3:
                    sp.dma_start(xreg[:, FEAT_COLS:TABLE_COLS],
                                 tables_in[:, FEAT_COLS:TABLE_COLS]).then_inc(s_tok, 16)
                sp.dma_start(x_tok[:, t, :], x_rows[t]).then_inc(s_x[t], 16)
            for t in range(2, SLOT_U):
                load("start", t, t)
            with sp.Fori(0, GROUPS - 1) as j:
                for n in range(2):
                    load("u", n, 2 * j + (SLOT_U + n))
            with sp.Fori(0, GROUPS) as j:
                for n in range(Z_PER):
                    load("z", n, Z_PER * j + (SLOT_Z + n))
            with sp.Fori(0, KT) as j:
                for n in range(2):
                    load("out0", n, 2 * j + (SLOT_OUT0 + n))
            with sp.Fori(0, HEADS) as h:
                for n in range(HEAD_PER):
                    load("head", n, HEAD_PER * h + (SLOT_HEAD + n))
            with sp.Fori(0, KT) as j:
                for n in range(2):
                    load("out1", n, 2 * j + (SLOT_OUT1 + n))
            for m in range(KT):
                if m < POOL_TILES:
                    sp.wait_ge(out_pool, m + 1)
                    src = tmp_t[:, m, 0:LAT]
                else:
                    sp.wait_ge(out_vec, m - POOL_TILES + 1)
                    src = x3[:, m, :]
                sp.dma_start(out[m], src).then_inc(s_out, 16)
            sp.wait_ge(s_out, 16 * KT)

        @block.gpsimd
        def _(pool):
            steps = [0]

            def link(instruction):
                steps[0] += 1
                instruction.then_inc(pool_step, 1)
                pool.wait_ge(pool_step, steps[0])

            def decay_first():
                d = [dk[:, i, :] for i in range(10)]
                tt = lambda o, a, b, op: link(pool.tensor_tensor(o, a, b, op))
                ts = lambda o, a, s1, s2, op0, op1: link(pool.tensor_scalar(o, a, s1, s2, op0, op1))
                ts(d[0], d[0], -126.0, 0.0, ALU.max, ALU.add)
                link(pool.tensor_copy(dki[:, :], d[0]))
                link(pool.tensor_copy(d[1], dki[:, :]))
                tt(d[2], d[0], d[1], ALU.subtract)
                ts(d[1], d[1], 127.0, 8388608.0, ALU.add, ALU.mult)
                link(pool.tensor_copy(dki[:, :], d[1]))
                ln2 = float(np.log(2.0))
                coef = [1.0]
                for i in range(1, 11):
                    coef.append(coef[-1] * ln2 / i)
                ts(d[3], d[2], coef[10], coef[9], ALU.mult, ALU.add)
                for i in range(8, -1, -1):
                    tt(d[3], d[3], d[2], ALU.mult)
                    ts(d[3], d[3], 1.0, coef[i], ALU.mult, ALU.add)
                tt(d[3], d[3], dki[:, :].bitcast(F32), ALU.mult)
                ts(d[4], d[3], -1.0, 2.0, ALU.mult, ALU.add)
                pool.tensor_scalar(d[7], d[3], -1.0, 1.0, ALU.mult, ALU.add).then_inc(rest_done, 1)

            def decay_second():
                d = [dk[:, i, :] for i in range(10)]
                tt = lambda o, a, b, op: link(pool.tensor_tensor(o, a, b, op))
                ts = lambda o, a, s1, s2, op0, op1: link(pool.tensor_scalar(o, a, s1, s2, op0, op1))
                pool.wait_ge(rest_done, 2)
                tt(d[4], d[4], d[3], ALU.mult)
                tt(d[5], d[4], d[4], ALU.mult)
                ts(d[6], d[5], 1.0 / 13, 1.0 / 11, ALU.mult, ALU.add)
                for i in (9, 7, 5, 3, 1):
                    tt(d[6], d[6], d[5], ALU.mult)
                    ts(d[6], d[6], 1.0, 1.0 / i, ALU.mult, ALU.add)
                tt(d[6], d[6], d[4], ALU.mult)
                ts(d[6], d[6], -2.0, 0.0, ALU.mult, ALU.add)
                pool.wait_ge(ln_done, 1)
                ts(d[5], d[3], 0.25, 0.0, ALU.is_gt, ALU.add)
                tt(d[7], d[7], d[6], ALU.subtract)
                tt(d[7], d[7], d[5], ALU.mult)
                tt(log_g, d[7], d[6], ALU.add)
                ts(dk[:, 8, :], log_g, -1.0, 0.0, ALU.mult, ALU.add)

            pool.memset(ones[:, :], 1.0).then_inc(ones_set, 1)
            pool.memset(ident4[:, :], 0.0).then_inc(ident4_set, 1)
            pool.wait_ge(ident4_set, 1)
            pool.affine_select(out=ident4[:, :], in_=ident4[:, :], compare_op=ALU.not_equal,
                               fill=1.0, base=0, pattern=[[-1, 4]],
                               channel_multiplier=1).then_inc(ident4_set, 1)
            pool.wait_ge(s_decay, 16)
            decay_first()
            pool.wait_ge(tab_hi, 1)
            pool.wait_ge(s_tok, 16)
            for a, b in ((FEAT_COLS, FEAT_COLS + 4 * NB), (FEAT_COLS + 4 * NB, TABLE_COLS)):
                pool.tensor_copy(tables[0][:, a:b], xreg[:, a:b]).then_inc(tab_hi, 1)
            pool.wait_ge(xs_lo, TT)
            pool.dma_start(tmp_t[:, :, 0:LAT],
                           x_lat.rearrange("p (k t) -> p k t", k=KT)).then_inc(s_xt, 16)
            pool.dma_start(tmp_t[:, :, LAT:TOK],
                           x_ctx.rearrange("p (k t) -> p k t", k=KT)).then_inc(s_xt, 16)

            def nyquist_weights(g):
                pool.wait_ge(wf_lo, KT * g + KT)
                for part in range(2):
                    pool.tensor_copy(nyq_w[part][:, :, g:g + 1],
                                     f32(wf[part][:, :, GDIM:GDIM + 1])).then_inc(nyq_copied, 1)

            nyquist_weights(0)
            pool.wait_ge(hf_lo, KT + 1)
            pool.memset(ident, 0.0).then_inc(ident_set, 1)
            pool.wait_ge(ident_set, 1)
            pool.affine_select(out=ident, in_=ident, compare_op=ALU.not_equal, fill=1.0, base=0,
                               pattern=[[-1, P]], channel_multiplier=1).then_inc(ident_set, 1)
            decay_second()
            pool.wait_ge(s_xt, 32)
            pool.wait_ge(rstd_row, 1)
            for k in range(KT):
                pool.tensor_tensor(tmp_t[:, k, :], tmp_t[:, k, :], rstd0, ALU.mult).then_inc(x_normed, 1)
                pool.wait_ge(x_normed, k + 1)
                for v, (a, b) in enumerate(((0, LAT), (LAT, TOK))):
                    pool.tensor_scalar(tmp_t[:, k, a:b], tmp_t[:, k, a:b], amul[:, 0, k, v:v + 1],
                                       mod0[:, k, v:v + 1], ALU.mult, ALU.add).then_inc(h_made, 1)
                if k < KT - 1:
                    nyquist_weights(k + 1)
            pool.wait_ge(nyq_vec, 1)

            def gate_group(p):
                for half in range(2):
                    pool.wait_ge(z_done, 4 * p + (2 * half + 2 + 8))
                    if half:
                        pool.wait_ge(gated, 8 * p + 4)
                        for i in range(2):
                            pool.dma_start(y3[0:1, p, NF * i:NF * i + NF],
                                           nyq_p[p:p + 1, :]).then_inc(s_row, 16)
                        pool.wait_ge(s_row, 32 * p + 32)
                    f = 2 * p + half
                    o, n = NF * half, NF * (1 - half)
                    for a, b, lo, size in ((0, HALF, 0, HALF), (HALF, LAT, HALF - 2, -1),
                                           (LAT, LAT + CHALF, HALF, CHALF),
                                           (LAT + CHALF, TOK, NF - 2, -1)):
                        if size > 0:
                            y = y3[:, p, o + lo:o + lo + size]
                        else:
                            y = y3[:, p, n + lo:n + lo - (b - a):-1]
                        g = gate0[:, f, a:b]
                        pool.tensor_tensor(g, y, g, ALU.mult).then_inc(gated, 1)

            for p in range(GROUPS):
                gate_group(p)
            pool.wait_ge(gated, 8 * GROUPS)
            pool.dma_start(xl, x_lat).then_inc(s_xl2, 16)
            pool.dma_start(xc, x_ctx).then_inc(s_xc2, 16)
            pool.wait_ge(rows_tr, CHUNKS + 1)
            pool.iota(dist[:, 0:896], pattern=[[1, 896]], base=-384, channel_multiplier=-1,
                      allow_small_or_imprecise_dtypes=True).then_inc(dist_set, 1)
            pool.wait_ge(glo, FT)
            pool.dma_start(gate[:, TAIL + 1536:TAIL + 2560], rope_in).then_inc(s_rope, 16)
            pool.wait_ge(rstd_done, 1)
            for k in (2, 5):
                pool.wait_ge(scaled, 2 * k + 1)
                pool.tensor_tensor(tmp_t[:, k, 0:LAT], tmp_t[:, k, 0:LAT], rstd_t[:, 0:LAT],
                                   ALU.mult).then_inc(t_pool, 1)
            pool.wait_ge(rstd_done, 2)
            for k in range(KT):
                pool.wait_ge(scaled, 2 * k + 2)
                pool.tensor_tensor(tmp_t[:, k, LAT:TOK], tmp_t[:, k, LAT:TOK], rstd_t[:, LAT:TOK],
                                   ALU.mult).then_inc(t_pool, 1)

            def norm_head(h):
                for i in range(1, 4):
                    pool.wait_ge(osq, 4 * h + i + 1)
                    if i > 1:
                        pool.wait_ge(oacc, 3 * h + i - 1)
                    pool.tensor_tensor(head_rstd, head_rstd, p_f[:, i % 2, :],
                                       ALU.add).then_inc(oacc, 1)

            def gate_head(h, tiles=range(4)):
                for i in tiles:
                    pool.wait_ge(onorm, 4 * h + i + 1)
                    g = one(gate1, 4 * h + i)
                    pool.tensor_tensor(g, g, p_f[:, i % 2, :], ALU.mult).then_inc(ogated, 1)

            def head(h, first):
                if not first:
                    norm_head(h - 1)
                def sums(n):
                    pool.wait_ge(turned, 8 * h + 4 * n + 4)
                    pool.tensor_tensor(turn[0], turn[0], turn[1],
                                       ALU.subtract).then_inc(summed, 1)
                    pool.tensor_tensor(turn[2], turn[2], turn[3], ALU.add).then_inc(summed, 1)
                sums(0)
                if not first:
                    gate_head(h - 1)
                sums(1)

            head(0, True)
            with pool.Fori(1, HEADS) as h:
                head(h, False)
            norm_head(HEADS - 1)
            gate_head(HEADS - 1, (0, 2))
            pool.wait_ge(rstd_done, 3)
            for m in range(POOL_TILES):
                pool.wait_ge(gained, m + 1)
                pool.tensor_tensor(tmp_t[:, m, 0:LAT], tmp_t[:, m, 0:LAT], rstd_t[:, 0:LAT],
                                   ALU.mult).then_inc(out_pool, 1)

        @block.scalar
        def _(act):
            def hi(phase, n, t, i=0, per=0):
                buf, landed = raw_at(phase, n)
                act.wait_ge(s_raw[buf], raw_step(phase, per) * i + landed if per else landed)
                for a in range(2):
                    c = slice(a * SLOT // 2, (a + 1) * SLOT // 2)
                    act.wait_ge(slot_done, 2 * t + (a + 1 - 4 + DONE0))
                    act.activation(ring[:, n % 2, 0, c], raw[:, buf, c], ACT.Copy).then_inc(hi_done, 1)

            def wf_hi_tiles(g, s):
                for r in range(4 * s, 4 * s + 4):
                    act.wait_ge(wf_mm, KT * g + r + 1)
                    act.activation(wf[0][:, r, :], bank(4 + r % 4, WCOLS), ACT.Copy).then_inc(wf_hi, 1)

            act.wait_ge(s_small, 16)
            act.activation(csf[:, :], small[:, 0:16], ACT.Silu).then_inc(csf_done, 1)
            act.wait_ge(s_feat, 16)
            act.activation(tables[0][:, 0:FEAT_COLS], xreg[:, 0:FEAT_COLS],
                           ACT.Copy).then_inc(tab_hi, 1)
            hi("start", 0, 0)
            hi("start", 1, 1)

            def x_root(t):
                act.wait_ge(s_x[t], 16)
                if t >= 2:
                    act.wait_ge(tok_sq, t - 1)
                act.activation(squares[:, t % 2, :], x_tok[:, t, :], ACT.Square,
                               accum_out=tok_ss[:, t:t + 1]).then_inc(tok_sq, 1)
                act.wait_ge(tok_sq, t + 1)
                act.activation(tok_rstd[:, t:t + 1], tok_ss[:, t:t + 1], ACT.Sqrt, scale=1.0 / D,
                               bias=eps[:, :]).then_inc(tok_root, 1)

            act.wait_ge(eps_set, 1)
            x_root(0)
            x_root(1)
            wf_hi_tiles(0, 0)
            wf_hi_tiles(0, 1)
            for t in range(2, TT):
                x_root(t)
                if t > 3:
                    act.wait_ge(tok_rstd_done, t)
                    act.activation(xs[0][:, t - 1, :], x_tok[:, t - 1, :], ACT.Copy,
                                   scale=tok_rstd[:, t - 1:t]).then_inc(xs_hi_act, 1)
            hi("start", 2, 2)
            hi("start", 3, 3)
            for k in range(KT):
                act.wait_ge(dft_done, k + 1)
                b = bank(2 * (k % 2) + 1)
                for dst, src, n in ((NF, 0, HALF - 2), (HALF, LAT // 2, CHALF),
                                    (NF + HALF - 2, LAT // 2 + CHALF, CHALF - 2)):
                    act.activation(xf[:, k, dst:dst + n], b[:, src:src + n],
                                   ACT.Copy).then_inc(sine_out, 1)
                if k < KT - 1:
                    hi("start", 2 * k + 4, 2 * k + 4)
                    hi("start", 2 * k + 5, 2 * k + 5)
            hi("u", 0, SLOT_U)
            hi("u", 1, SLOT_U + 1)
            act.wait_ge(mods, 1)
            act.wait_ge(cosine_out, KT)
            act.wait_ge(sine_out, 3 * KT)
            for k in range(KT):
                for v, kind, a, src, n in TRANSFORM_PARTS:
                    act.activation(hf[0][kind][:, k, a:a + n], xf[:, k, src:src + n], ACT.Copy,
                                   scale=amul[:, 0, k, v:v + 1]).then_inc(hf_hi, 1)

            def copy_q(g):
                act.wait_ge(u_done, g + 1)
                act.wait_ge(ds_done, 2 * g + 2)
                act.activation(q_f, bank(1, NF), ACT.Copy).then_inc(q_copied, 1)

            act.sem_inc(z_done, 8)
            act.wait_ge(rest_done, 1)
            act.activation(dk[:, 7, :], dk[:, 7, :], ACT.Ln).then_inc(ln_done, 1)

            def u_group(g, n, phase, i=0, per=0):
                copy_q(g)
                act.wait_ge(nyq_copied, 2 * g + 2)
                wf_hi_tiles(g + 1, 0)
                hi(phase, n, 2 * g + (SLOT_U + 2), i, per)
                wf_hi_tiles(g + 1, 1)
                hi(phase, n + 1, 2 * g + (SLOT_U + 3), i, per)

            u_group(0, 2, "u")
            act.wait_ge(rstd_row_mm, 1)
            act.activation(rstd0, banks[:, 2 * 512:2 * 512 + TOK], ACT.Copy).then_inc(rstd_row, 1)
            with act.Fori(1, GROUPS - 2) as g:
                u_group(g, 2, "u", g, 2)
            u_group(GROUPS - 2, 0, "z")
            copy_q(GROUPS - 1)
            act.wait_ge(nyq_mm, 1)
            for k in range(KT):
                act.wait_ge(h_made, 2 * k + 2)
                act.activation(h_hi[:, k, :], tmp_t[:, k, :], ACT.Copy).then_inc(hhi_done, 1)

            def g_hi(kk):
                act.wait_ge(gated, 8 * (kk // 2) + 8)
                act.activation(g0(kk, 0), gate0[:, kk, :], ACT.Copy).then_inc(ghi, 1)

            def gates(jj, q, split=None, last=False):
                j = 2 * jj + q
                for n in range(2, Z_PER + 2):
                    if last and n >= Z_PER:
                        hi("out0", n - Z_PER, SLOT_OUT0 + n - Z_PER)
                    else:
                        hi("z", Z_PER * q + n, Z_PER * j + (SLOT_Z + n), jj, 2 * Z_PER)
                for half in range(2):
                    for a, b, src in ((0, LAT, bank(3 * q + half)),
                                      (LAT, TOK, bank(3 * q + 2, CTX, CTX * half))):
                        act.activation(one(gate0[:, :, a:b], 2 * j + half), src,
                                       ACT.Silu).then_inc(z_done, 1)
                if split is not None:
                    act.wait_ge(gated, 8 * split + 8)
                    for half in range(2):
                        act.activation(g0_hi_at(2 * split + half), one(gate0, 2 * split + half),
                                       ACT.Copy).then_inc(ghi, 1)

            gates(0, 0)
            gates(0, 1)
            with act.Fori(1, 3) as jj:
                gates(jj, 0, 2 * jj - 2)
                gates(jj, 1, 2 * jj - 1)
            gates(3, 0)
            gates(3, 1, last=True)

            for kk in range(8, 14):
                g_hi(kk)
            hi("out0", 2, SLOT_OUT0 + 2)
            hi("out0", 3, SLOT_OUT0 + 3)
            g_hi(14)
            g_hi(15)
            hi("out0", 4, SLOT_OUT0 + 4)
            hi("out0", 5, SLOT_OUT0 + 5)

            def x1_tile(m, q):
                for v, (a, b, x) in enumerate(((0, LAT, x3), (LAT, TOK, xc3))):
                    act.wait_ge(x1_done, 2 * m + (v + 1 + 4))
                    act.wait_ge(acc_done, 2 * m + (v + 1))
                    act.activation(sq_t[:, q, a:b], one(x, m), ACT.Square).then_inc(sq_done, 1)
                    act.activation(one(tmp_t[:, :, a:b], m), one(x, m), ACT.Copy,
                                   scale=one(amul[:, 1, :, v:v + 1], m)).then_inc(scaled, 1)

            act.wait_ge(mods, 2)
            act.wait_ge(glo, FT)
            x1_tile(0, 0)
            x1_tile(1, 1)
            with act.Fori(1, 3) as jj:
                for q in range(2):
                    hi("out0", 4 + 2 * q + 2 - 4, 4 * jj + (SLOT_OUT0 + 2 * q + 2), jj, 4)
                    hi("out0", 4 + 2 * q + 3 - 4, 4 * jj + (SLOT_OUT0 + 2 * q + 3), jj, 4)
                    x1_tile(2 * jj + q, q)
            hi("out0", 14, SLOT_OUT0 + 14)
            hi("out0", 15, SLOT_OUT0 + 15)
            x1_tile(6, 0)
            act.activation(dk[:, 1, 0:1], eps[:, :], ACT.Sqrt).then_inc(warm, 1)
            hi("head", 0, SLOT_HEAD)
            hi("head", 1, SLOT_HEAD + 1)
            x1_tile(7, 1)

            def root(n, a, b):
                act.wait_ge(sum_sq_done, n + 1)
                act.activation(rstd_t[:, a:b], banks[:, a:b], ACT.Sqrt, scale=1.0 / D,
                               bias=eps[:, :]).then_inc(root_done, 1)

            def h1_hi(k, v, a, b):
                if v == 0 and k not in (2, 5):
                    act.wait_ge(t_vec, [0, 1, 3, 4, 6, 7].index(k) + 1)
                else:
                    act.wait_ge(t_pool, (2, 5).index(k) + 1 if v == 0 else k + 3)
                act.activation(h_hi[:, k, a:b], tmp_t[:, k, a:b], ACT.Identity,
                               bias=mod1[:, 8 + k, v:v + 1]).then_inc(hhi_done, 1)

            root(0, 0, LAT)
            root(1, LAT, TOK)
            for k in range(KT):
                h1_hi(k, 0, 0, LAT)
            for k in range(KT):
                h1_hi(k, 1, LAT, TOK)

            def o_squares(h):
                for i in range(4):
                    act.wait_ge(pv_done, 6 * h + 6)
                    if i == 3:
                        act.wait_ge(oacc, 3 * h + 1)
                    dst = head_rstd if i == 0 else p_f[:, i % 2, :]
                    act.activation(dst, bank(2 + i), ACT.Square).then_inc(osq, 1)

            def o_root(h):
                act.wait_ge(oss, h + 1)
                act.activation(head_rstd, bank(6), ACT.Sqrt, scale=1.0 / DV,
                               bias=eps[:, :]).then_inc(oroot, 1)

            def g1_hi(kk):
                if kk >= 12 and kk % 2 == 0:
                    act.wait_ge(ogated, 13 + (kk - 12) // 2)
                elif kk >= 12:
                    act.wait_ge(vec_gated, 1 + (kk - 12) // 2)
                act.activation(g1(kk, 0), gate1[:, kk, :], ACT.Copy).then_inc(ghi, 1)

            def head(h, first=False, last=False):
                def used(s):
                    if last and s + 2 >= HEAD_PER:
                        hi("out1", s + 2 - HEAD_PER, SLOT_OUT1 + s + 2 - HEAD_PER)
                    else:
                        hi("head", s + 2, HEAD_PER * h + (SLOT_HEAD + s + 2), h, HEAD_PER)

                def turned_hi(n, dst):
                    for i in range(2):
                        act.wait_ge(summed, 4 * h + 2 * n + i + 1)
                        act.activation(dst[:, i, 0:LAT], turn[2 * i],
                                       ACT.Copy).then_inc(qkhi, 1)

                def silu(i, b):
                    act.activation(one(gate1, 4 * h + i), bank(b), ACT.Silu).then_inc(z1_done, 1)

                used(0)
                if not first:
                    o_root(h - 1)
                used(1)
                turned_hi(0, q_s[0])
                used(2)
                used(3)
                silu(0, 7)
                silu(1, 6)
                used(4)
                used(5)
                act.activation(k_s[0][:, 0, LAT:TOK], bank(3, CTX), ACT.Copy).then_inc(qkhi, 1)
                act.activation(k_s[0][:, 1, LAT:TOK], bank(5, CTX), ACT.Copy).then_inc(qkhi, 1)
                turned_hi(1, k_s[0])
                used(6)
                silu(2, 7)
                used(7)
                act.wait_ge(expo_done, 5 * h + 2)
                act.activation(strip_ctx, strip_ctx, ACT.Exp).then_inc(exp_done, 1)
                act.activation(dexp[:, 0:640], dexp[:, 0:640], ACT.Exp).then_inc(exp_done, 1)
                used(8)
                act.wait_ge(expo_done, 5 * h + 5)
                act.activation(strip_lat, strip_lat, ACT.Exp).then_inc(exp_done, 1)
                used(9)
                used(10)
                for t in range(TT):
                    act.activation(v_s[0][:, t, :], bank(V_BANK[t]), ACT.Copy).then_inc(vhi, 1)
                if last:
                    act.wait_ge(ogated, 12)
                for t in range(TT):
                    if t == 2:
                        used(11)
                        silu(3, 0)
                    act.wait_ge(pf_done, 6 * h + t + 1)
                    if t >= 2:
                        act.wait_ge(pv_done, 6 * h + t - 1)
                    act.activation(p_s[0][:, t % 2, :], p_f[:, t % 2, :],
                                   ACT.Copy).then_inc(phi, 1)
                    if last and t >= 2:
                        g1_hi(2 * t - 4)
                        g1_hi(2 * t - 3)

            head(0, first=True)
            with act.Fori(1, HEADS - 1) as h:
                o_squares(h - 1)
                head(h)
            o_squares(HEADS - 2)
            head(HEADS - 1, last=True)
            act.activation(dk[:, 1, 0:1], eps[:, :], ACT.Sqrt).then_inc(warm, 1)
            o_squares(HEADS - 1)
            for kk in range(8, 12):
                g1_hi(kk)
            o_root(HEADS - 1)
            hi("out1", 2, SLOT_OUT1 + 2)
            hi("out1", 3, SLOT_OUT1 + 3)
            for kk in range(12, FT):
                g1_hi(kk)
            hi("out1", 4, SLOT_OUT1 + 4)
            hi("out1", 5, SLOT_OUT1 + 5)

            def x2_sq(m, q):
                act.wait_ge(x1_done, m + (2 * KT + 1 + 4))
                act.wait_ge(acc_done, m + (2 * KT + 4))
                act.activation(sq_t[:, q, 0:LAT], one(x3, m), ACT.Square).then_inc(sq_done, 1)

            x2_sq(0, 0)
            x2_sq(1, 1)
            with act.Fori(1, 3) as jj:
                for q in range(2):
                    hi("out1", 2 * q + 2, 4 * jj + (SLOT_OUT1 + 2 * q + 2), jj, 4)
                    hi("out1", 2 * q + 3, 4 * jj + (SLOT_OUT1 + 2 * q + 3), jj, 4)
                    x2_sq(2 * jj + q, q)
            hi("out1", 14, SLOT_OUT1 + 14)
            hi("out1", 15, SLOT_OUT1 + 15)
            x2_sq(6, 0)
            for m in range(POOL_TILES):
                act.activation(tmp_t[:, m, 0:LAT], x3[:, m, :], ACT.Copy,
                               scale=g_final[:, m:m + 1]).then_inc(gained, 1)
            act.activation(dk[:, 1, 0:1], eps[:, :], ACT.Sqrt).then_inc(warm, 1)
            x2_sq(7, 1)
            act.wait_ge(sum_sq_done, 3)
            act.activation(rstd_t[:, 0:LAT], bank(0), ACT.Sqrt, scale=1.0 / D,
                           bias=eps[:, :]).then_inc(root_done, 1)

        @block.vector
        def _(dve):
            steps = [0]

            def link(instruction):
                steps[0] += 1
                instruction.then_inc(step, 1)
                dve.wait_ge(step, steps[0])

            def lo(phase, n, t):
                buf = raw_at(phase, n)[0]
                for a in range(2):
                    c = slice(a * SLOT // 2, (a + 1) * SLOT // 2)
                    dve.wait_ge(hi_done, 2 * t + (a + 1))
                    dve.tensor_tensor(ring[:, n % 2, 1, c], raw[:, buf, c],
                                      f32(ring[:, n % 2, 0, c]), ALU.subtract).then_inc(split_done, 1)

            def wf_lo_tiles(g, s):
                for r in range(4 * s, 4 * s + 4):
                    dve.wait_ge(wf_hi, KT * g + r + 1)
                    dve.tensor_tensor(wf[1][:, r, :], bank(4 + r % 4, WCOLS), f32(wf[0][:, r, :]),
                                      ALU.subtract).then_inc(wf_lo, 1)

            def table_lo(n, a, b):
                dve.wait_ge(tab_hi, n)
                dve.tensor_tensor(tables[1][:, a:b], xreg[:, a:b], f32(tables[0][:, a:b]),
                                  ALU.subtract).then_inc(tab_lo, 1)

            def copy_rows(c, used):
                dve.wait_ge(slot_done, 2 * used + (2 + DONE0))
                dve.wait_ge(rows_tr, c + 1)
                dve.tensor_copy(rows, bank(7, parts=4)).then_inc(rows_done, 1)

            def copy_mod(c):
                dve.wait_ge(rows_tr, c + 2)
                dve.tensor_copy(mod_t[:, bass.ds(4 * c, 4), :],
                                bank(6, 16).rearrange("p (t r) -> p t r", t=4)).then_inc(mod_copied, 1)

            def columns(mod, first, n, biases):
                link(dve.tensor_tensor(mod, mod_t[:, first:first + n, 0:4:2],
                                       mod_t[:, first:first + n, 1:4:2], ALU.add))
                for a, b, bias in biases:
                    link(dve.tensor_tensor(mod[:, a:b, :], mod[:, a:b, :],
                                           bias.unsqueeze(2).to_broadcast([P, b - a, 2]), ALU.add))

            def multiplier(layer, scale):
                g = g_norm[layer].unsqueeze(2).to_broadcast([P, KT, 2])
                link(dve.tensor_scalar(scale, scale, 1.0, 0.0, ALU.add, ALU.add))
                dve.tensor_tensor(amul[:, layer, :, :], scale, g, ALU.mult).then_inc(mods, 1)

            dve.sem_inc(split_done, SPLIT0)
            dve.sem_inc(rows_tr, 1)
            dve.sem_inc(ds_done, 2)
            dve.sem_inc(x1_done, 4)
            dve.sem_inc(acc_done, 3)
            dve.memset(eps[:, :], EPS).then_inc(eps_set, 1)
            dve.wait_ge(csf_done, 1)
            for v in range(2):
                c = csf[:, KT * v:KT * v + KT]
                link(dve.tensor_copy(cond[:, :, 2 * v], c))
                dve.tensor_tensor(cond[:, :, 2 * v + 1], c, f32(cond[:, :, 2 * v]),
                                  ALU.subtract).then_inc(cond_done, 1)
            table_lo(1, 0, FEAT_COLS)
            lo("start", 0, 0)
            lo("start", 1, 1)

            def x_rstd(t):
                dve.wait_ge(tok_root, t + 1)
                dve.reciprocal(tok_rstd[:, t:t + 1], tok_rstd[:, t:t + 1]).then_inc(tok_rstd_done, 1)

            x_rstd(0)
            x_rstd(1)
            wf_lo_tiles(0, 0)
            wf_lo_tiles(0, 1)
            for t in range(TT):
                if 1 <= t < TT - 1:
                    x_rstd(t + 1)
                dve.wait_ge(tok_rstd_done, t + 1)
                if t in (3, 4):
                    dve.wait_ge(xs_hi_act, t - 2)
                else:
                    dve.tensor_scalar(xs[0][:, t, :], x_tok[:, t, :], tok_rstd[:, t:t + 1], None,
                                      ALU.mult).then_inc(xs_hi, 1)
                    dve.wait_ge(xs_hi, min(t + 1, 4))
                dve.scalar_tensor_tensor(out=xs[1][:, t, :], in0=x_tok[:, t, :],
                                         scalar=tok_rstd[:, t:t + 1], in1=f32(xs[0][:, t, :]),
                                         op0=ALU.mult, op1=ALU.subtract).then_inc(xs_lo, 1)
                if t == 3:
                    table_lo(2, FEAT_COLS, FEAT_COLS + 4 * NB)
                if t == 4:
                    table_lo(3, FEAT_COLS + 4 * NB, TABLE_COLS)
            lo("start", 2, 2)
            lo("start", 3, 3)
            dve.wait_ge(rest_done, 1)
            dve.reciprocal(dk[:, 4, :], dk[:, 4, :]).then_inc(rest_done, 1)
            for k in range(KT):
                dve.wait_ge(dft_done, k + 1)
                dve.tensor_copy(xf[:, k, 0:HALF], bank(2 * (k % 2), HALF)).then_inc(cosine_out, 1)
                if k % 2 == 0 and k > 0:
                    copy_mod(k // 2 - 1)
                if k < KT - 1:
                    lo("start", 2 * k + 4, 2 * k + 4)
                    lo("start", 2 * k + 5, 2 * k + 5)
                if k % 2:
                    copy_rows(k // 2, 2 * k + 3)
            copy_mod(3)
            dve.wait_ge(mod_copied, 5)
            columns(mod0[:, :, :], 0, 16, ((0, 16, bias0[:, 0:16]),))
            multiplier(0, mod0[:, 8:16, :])
            ends = slice(0, HALF + 1, HALF)
            dve.wait_ge(mods, 1)
            dve.wait_ge(cosine_out, KT)
            dve.wait_ge(sine_out, 3 * KT)
            link(dve.tensor_tensor(shift0, xf[:, :, ends], amul[:, 0, :, :], ALU.mult))
            for v, tokens in ((0, LAT), (1, CTX)):
                link(dve.scalar_tensor_tensor(out=shift0[:, :, v], in0=mod0[:, 0:KT, v],
                                              scalar=float(np.sqrt(tokens)), in1=shift0[:, :, v],
                                              op0=ALU.mult, op1=ALU.add))
            dve.wait_ge(dft_done, KT)
            link(dve.tensor_copy(hf[0][0][:, :, ends], shift0))
            dve.tensor_tensor(hf[1][0][:, :, ends], shift0, f32(hf[0][0][:, :, ends]),
                              ALU.subtract).then_inc(shift_done, 1)
            for part in range(2):
                for zeros in (slice(0, HALF, HALF - 1), slice(HALF, NF, CHALF - 1)):
                    dve.tensor_scalar(hf[part][1][:, :, zeros], f32(xf[:, :, zeros]), 0.0, None,
                                      ALU.mult).then_inc(shift_done, 1)
            n = 0
            for k in range(KT):
                for v, kind, a, src, size in TRANSFORM_PARTS:
                    n += 1
                    dve.wait_ge(hf_hi, n)
                    dve.scalar_tensor_tensor(out=hf[1][kind][:, k, a:a + size],
                                             in0=xf[:, k, src:src + size],
                                             scalar=amul[:, 0, k, v:v + 1],
                                             in1=f32(hf[0][kind][:, k, a:a + size]), op0=ALU.mult,
                                             op1=ALU.subtract).then_inc(hf_lo, 1)
            lo("u", 0, SLOT_U)
            lo("u", 1, SLOT_U + 1)

            def sum_diff(g):
                dve.wait_ge(q_copied, g + 1)
                for i, op in enumerate((ALU.subtract, ALU.add)):
                    dve.tensor_tensor(one(y3[:, :, NF * i:NF * i + NF], g), bank(0, NF), q_f,
                                      op).then_inc(ds_done, 1)

            def u_group(g, n, phase):
                sum_diff(g)
                wf_lo_tiles(g + 1, 0)
                lo(phase, n, 2 * g + (SLOT_U + 2))
                wf_lo_tiles(g + 1, 1)
                lo(phase, n + 1, 2 * g + (SLOT_U + 3))

            dve.wait_ge(ident_set, 2)
            for t in range(TT):
                dve.tensor_scalar(diag[:, t, :], ident, tok_rstd[:, t:t + 1], None,
                                  ALU.mult).then_inc(diag_done, 1)
            u_group(0, 0, "u")
            with dve.Fori(1, GROUPS - 2) as g:
                u_group(g, 0, "u")
            u_group(GROUPS - 2, 0, "z")
            sum_diff(GROUPS - 1)
            dve.wait_ge(nyq_mm, 1)
            dve.tensor_copy(nyq_p, bank(2, NF, parts=GROUPS)).then_inc(nyq_vec, 1)
            for k in range(KT):
                dve.wait_ge(hhi_done, k + 1)
                dve.tensor_tensor(h_lo[:, k, :], tmp_t[:, k, :], f32(h_hi[:, k, :]),
                                  ALU.subtract).then_inc(hlo_done, 1)

            def gates(jj, q, split=None, first=False, last=False):
                j = 2 * jj + q
                for n in range(2, Z_PER + 2):
                    if last and n >= Z_PER:
                        lo("out0", n - Z_PER, SLOT_OUT0 + n - Z_PER)
                    else:
                        lo("z", Z_PER * q + n, Z_PER * j + (SLOT_Z + n))
                    if n == Z_PER:
                        copy_rows(j + 4, Z_PER * j + (SLOT_Z + Z_PER - 1))
                if not first:
                    copy_mod(j + 3)
                if split is not None:
                    for half in range(2):
                        kk = 2 * split + half
                        dve.wait_ge(ghi, kk + 1)
                        dve.tensor_tensor(g0_lo_at(kk), one(gate0, kk), f32(g0_hi_at(kk)),
                                          ALU.subtract).then_inc(glo, 1)

            gates(0, 0, first=True)
            gates(0, 1)
            with dve.Fori(1, 3) as jj:
                gates(jj, 0, 2 * jj - 2)
                gates(jj, 1, 2 * jj - 1)
            gates(3, 0)
            gates(3, 1, last=True)

            def g_lo(kk):
                dve.wait_ge(ghi, kk + 1)
                dve.tensor_tensor(g0(kk, 1), gate0[:, kk, :], f32(g0(kk, 0)),
                                  ALU.subtract).then_inc(glo, 1)

            for kk in range(8, 14):
                g_lo(kk)
            copy_mod(CHUNKS - 1)
            lo("out0", 2, SLOT_OUT0 + 2)
            lo("out0", 3, SLOT_OUT0 + 3)
            dve.wait_ge(mod_copied, CHUNKS + 1)
            columns(mod1[:, :, :], 16, 4 * KT, ((0, KT, bias0[:, 16:24]), (KT, 4 * KT, bias1)))
            multiplier(1, mod1[:, 2 * KT:3 * KT, :])
            g_lo(14)
            g_lo(15)
            lo("out0", 4, SLOT_OUT0 + 4)
            lo("out0", 5, SLOT_OUT0 + 5)
            dve.wait_ge(glo, FT)
            dve.memset(acc_t, 0.0).then_inc(acc_done, 1)
            dve.wait_ge(s_xl2, 16)
            dve.wait_ge(s_xc2, 16)

            def x1_tile(m, banks_lc, used):
                dve.wait_ge(slot_done, 2 * used + (2 + DONE0))
                for v, x in enumerate((x3, xc3)):
                    dve.scalar_tensor_tensor(out=one(x, m), in0=banks_lc[v],
                                             scalar=one(mod1[:, :, v:v + 1], m), in1=one(x, m),
                                             op0=ALU.mult, op1=ALU.add).then_inc(x1_done, 1)

            def x1_squares(m, q):
                for v, (a, b) in enumerate(((0, LAT), (LAT, TOK))):
                    dve.wait_ge(sq_done, 2 * m + (v + 1))
                    dve.wait_ge(acc_done, 2 * m + (v + 3))
                    dve.tensor_tensor(acc_t[:, a:b], acc_t[:, a:b], sq_t[:, q, a:b],
                                      ALU.add).then_inc(acc_done, 1)

            for m in range(2):
                x1_tile(m, (bank(m), bank(2, CTX, CTX * m)), SLOT_OUT0 + 3)
            for m in range(2):
                x1_squares(m, m)
            with dve.Fori(1, 3) as jj:
                for q in range(2):
                    lo("out0", 2 * q + 2, 4 * jj + (SLOT_OUT0 + 2 * q + 2))
                    lo("out0", 2 * q + 3, 4 * jj + (SLOT_OUT0 + 2 * q + 3))
                    x1_tile(2 * jj + q, (bank(3 + 2 * q), bank(4 + 2 * q, CTX)),
                            4 * jj + (SLOT_OUT0 + 2 * q + 1))
                    x1_squares(2 * jj + q, q)
            for q in range(2):
                if q == 0:
                    lo("out0", 14, SLOT_OUT0 + 14)
                    lo("out0", 15, SLOT_OUT0 + 15)
                else:
                    lo("head", 0, SLOT_HEAD)
                x1_tile(6 + q, (bank(3 + 2 * q), bank(4 + 2 * q, CTX)), SLOT_OUT0 + 13 + 2 * q)
                x1_squares(6 + q, q)
            lo("head", 1, SLOT_HEAD + 1)
            dve.wait_ge(root_done, 1)
            dve.reciprocal(rstd_t[:, 0:LAT], rstd_t[:, 0:LAT]).then_inc(rstd_done, 1)
            dve.wait_ge(rstd_done, 1)

            def h1_norm(k):
                if k < KT and k not in (2, 5):
                    dve.wait_ge(scaled, 2 * k + 1)
                    dve.tensor_tensor(tmp_t[:, k, 0:LAT], tmp_t[:, k, 0:LAT], rstd_t[:, 0:LAT],
                                      ALU.mult).then_inc(t_vec, 1)

            def h1_low(k, v, a, b):
                dve.wait_ge(hhi_done, KT * (v + 1) + k + 1)
                dve.scalar_tensor_tensor(out=h_lo[:, k, a:b], in0=tmp_t[:, k, a:b],
                                         scalar=mod1[:, 8 + k, v:v + 1], in1=f32(h_hi[:, k, a:b]),
                                         op0=ALU.add, op1=ALU.subtract).then_inc(hlo_done, 1)

            h1_norm(0)
            h1_norm(1)
            for k in range(KT):
                if k == 1:
                    dve.wait_ge(root_done, 2)
                    dve.reciprocal(rstd_t[:, LAT:TOK], rstd_t[:, LAT:TOK]).then_inc(rstd_done, 1)
                h1_norm(k + 2)
                h1_low(k, 0, 0, LAT)
            for k in range(KT):
                h1_low(k, 1, LAT, TOK)

            def o_rstd(h):
                dve.wait_ge(oroot, h + 1)
                dve.reciprocal(head_rstd, head_rstd).then_inc(orstd, 1)

            def o_norm(h, first, end):
                dve.wait_ge(orstd, h + 1)
                for i in range(first, end):
                    if i >= 2:
                        dve.wait_ge(ogated, 4 * h + i - 1)
                    dve.tensor_tensor(p_f[:, i % 2, :], bank(2 + i), head_rstd,
                                      ALU.mult).then_inc(onorm, 1)

            def last_norm():
                dve.wait_ge(orstd, HEADS)
                for i in range(4):
                    if i == 2:
                        dve.wait_ge(ogated, FT - 3)
                    if i == 3:
                        dve.wait_ge(vec_gated, 1)
                    dve.tensor_tensor(p_f[:, i % 2, :], bank(2 + i), head_rstd,
                                      ALU.mult).then_inc(onorm, 1)
                    if i % 2:
                        dve.wait_ge(onorm, FT - 3 + i)
                        dve.tensor_tensor(gate1[:, FT - 4 + i, :], gate1[:, FT - 4 + i, :],
                                          p_f[:, 1, :], ALU.mult).then_inc(vec_gated, 1)

            def g1_lo(kk):
                dve.wait_ge(ghi, FT + kk + 1)
                dve.tensor_tensor(g1(kk, 1), gate1[:, kk, :], f32(g1(kk, 0)),
                                  ALU.subtract).then_inc(glo, 1)

            def head(h, first=False, last=False):
                lf, nlb = dk[:, 9, bass.ds(h, 1)], dk[:, 8, bass.ds(h + 4, 1)]

                def used(s):
                    if last and s + 2 >= HEAD_PER:
                        lo("out1", s + 2 - HEAD_PER, SLOT_OUT1 + s + 2 - HEAD_PER)
                    else:
                        lo("head", s + 2, HEAD_PER * h + (SLOT_HEAD + s + 2))

                def turns(n, a, b):
                    for dst, src, w in ((0, a, cos_t), (1, b, sin_t), (2, a, sin_t), (3, b, cos_t)):
                        dve.tensor_tensor(turn[dst], bank(src), w, ALU.mult).then_inc(turned, 1)

                def part_lo(n, dst, src):
                    dve.wait_ge(qkhi, 6 * h + n)
                    dve.tensor_tensor(dst[1], src, f32(dst[0]), ALU.subtract).then_inc(qklo, 1)

                def both(t, i, a, b):
                    return t[0][:, i, a:b], t[1][:, i, a:b]

                used(0)
                if not first:
                    o_rstd(h - 1)
                used(1)
                turns(0, 0, 1)
                if not first:
                    o_norm(h - 1, 0, 2)
                part_lo(1, both(q_s, 0, 0, LAT), turn[0])
                part_lo(2, both(q_s, 1, 0, LAT), turn[2])
                if not first:
                    o_norm(h - 1, 2, 4)
                used(2)
                used(3)
                used(4)
                used(5)
                part_lo(3, both(k_s, 0, LAT, TOK), bank(3, CTX))
                dve.wait_ge(qklo, 6 * h + 2)
                turns(1, 2, 4)
                part_lo(4, both(k_s, 1, LAT, TOK), bank(5, CTX))
                part_lo(5, both(k_s, 0, 0, LAT), turn[0])
                part_lo(6, both(k_s, 1, 0, LAT), turn[2])
                used(6)
                dve.wait_ge(qklo, 6 * h + 6)
                dve.tensor_scalar(strip_ctx, dist[:, 0:640], float(LAT), lf, ALU.add,
                                  ALU.mult).then_inc(expo_done, 1)
                dve.tensor_scalar(dexp[:, 0:640], dist[:, 0:640], float(LAT - TOK), nlb, ALU.add,
                                  ALU.mult).then_inc(expo_done, 1)
                used(7)
                dve.wait_ge(exp_done, 3 * h + 2)
                dve.tensor_tensor(strip_ctx, strip_ctx, dexp[:, 0:640],
                                  ALU.add).then_inc(strip_done, 1)
                dve.wait_ge(strip_done, 2 * h + 1)
                dve.tensor_scalar(dexp, dist[:, 0:896], 0.0, nlb, ALU.min, ALU.mult).then_inc(expo_done, 1)
                dve.tensor_scalar(strip_lat, dist[:, 0:896], 0.0, lf, ALU.max, ALU.mult).then_inc(expo_done, 1)
                dve.wait_ge(expo_done, 5 * h + 4)
                dve.tensor_tensor(strip_lat, strip_lat, dexp, ALU.add).then_inc(expo_done, 1)
                used(8)
                dve.wait_ge(exp_done, 3 * h + 3)
                dve.scalar_tensor_tensor(out=strip_lat, in0=dist[:, 0:896], scalar=0.0, in1=strip_lat,
                                         op0=ALU.is_equal, op1=ALU.add).then_inc(strip_done, 1)
                used(9)
                used(10)
                for t in range(TT):
                    dve.wait_ge(vhi, 6 * h + t + 1)
                    dve.tensor_tensor(v_s[1][:, t, :], bank(V_BANK[t]), f32(v_s[0][:, t, :]),
                                      ALU.subtract).then_inc(vlo, 1)
                dve.wait_ge(strip_done, 2 * h + 2)

                def decayed(t):
                    strip = (strip_lat[:, 384 - P * t:384 - P * t + LAT] if t < 4 else
                             strip_ctx[:, P * (5 - t):P * (5 - t) + LAT])
                    dve.wait_ge(score_done, 6 * h + t + 1)
                    if t >= 2:
                        dve.wait_ge(plo, 6 * h + t - 1)
                    dve.scalar_tensor_tensor(out=p_f[:, t % 2, :], in0=bank(6 + t % 2),
                                             scalar=QK ** -0.5, in1=strip, op0=ALU.mult,
                                             op1=ALU.mult).then_inc(pf_done, 1)

                if not first:
                    dve.wait_ge(ogated, 4 * h)
                decayed(0)
                decayed(1)
                for t in range(TT):
                    if t == 2:
                        used(11)
                    if t >= 2:
                        decayed(t)
                    dve.wait_ge(phi, 6 * h + t + 1)
                    dve.tensor_tensor(p_s[1][:, t % 2, :], p_f[:, t % 2, :], f32(p_s[0][:, t % 2, :]),
                                      ALU.subtract).then_inc(plo, 1)
                    if last and t >= 2:
                        g1_lo(2 * t - 4)
                        g1_lo(2 * t - 3)

            dve.wait_ge(s_rope, 16)
            dve.wait_ge(dist_set, 1)
            head(0, first=True)
            with dve.Fori(1, HEADS - 1) as h:
                head(h)
            head(HEADS - 1, last=True)
            for kk in range(8, 12):
                g1_lo(kk)
            o_rstd(HEADS - 1)
            last_norm()
            lo("out1", 2, SLOT_OUT1 + 2)
            lo("out1", 3, SLOT_OUT1 + 3)
            for kk in range(12, FT):
                g1_lo(kk)
            lo("out1", 4, SLOT_OUT1 + 4)
            lo("out1", 5, SLOT_OUT1 + 5)
            dve.wait_ge(ogated, FT - 2)
            dve.wait_ge(vec_gated, 2)
            dve.memset(acc_t[:, 0:LAT], 0.0).then_inc(acc_done, 1)

            def x2_tile(m, b, used):
                dve.wait_ge(slot_done, 2 * used + (2 + DONE0))
                dve.scalar_tensor_tensor(out=one(x3, m), in0=bank(b),
                                         scalar=one(mod1[:, :, 0:1], m + 24), in1=one(x3, m),
                                         op0=ALU.mult, op1=ALU.add).then_inc(x1_done, 1)

            def x2_squares(m, q):
                dve.wait_ge(sq_done, m + (2 * KT + 1))
                dve.wait_ge(acc_done, m + (2 * KT + 5))
                dve.tensor_tensor(acc_t[:, 0:LAT], acc_t[:, 0:LAT], sq_t[:, q, 0:LAT],
                                  ALU.add).then_inc(acc_done, 1)

            for m in range(2):
                x2_tile(m, m, SLOT_OUT1 + 3)
            for m in range(2):
                x2_squares(m, m)
            with dve.Fori(1, 3) as jj:
                for q in range(2):
                    lo("out1", 2 * q + 2, 4 * jj + (SLOT_OUT1 + 2 * q + 2))
                    lo("out1", 2 * q + 3, 4 * jj + (SLOT_OUT1 + 2 * q + 3))
                    x2_tile(2 * jj + q, 7 - q, 4 * jj + (SLOT_OUT1 + 2 * q + 1))
                    x2_squares(2 * jj + q, q)
            for q in range(2):
                if q == 0:
                    lo("out1", 14, SLOT_OUT1 + 14)
                    lo("out1", 15, SLOT_OUT1 + 15)
                x2_tile(6 + q, 7 - q, SLOT_OUT1 + 13 + 2 * q)
                x2_squares(6 + q, q)
            dve.wait_ge(root_done, 3)
            dve.reciprocal(rstd_t[:, 0:LAT], rstd_t[:, 0:LAT]).then_inc(rstd_done, 1)
            dve.wait_ge(rstd_done, 3)
            for m in range(POOL_TILES, KT):
                dve.scalar_tensor_tensor(out=x3[:, m, :], in0=x3[:, m, :], scalar=g_final[:, m:m + 1],
                                         in1=rstd_t[:, 0:LAT], op0=ALU.mult,
                                         op1=ALU.mult).then_inc(out_vec, 1)

        @block.tensor
        def _(pe):
            def mm3(out, left, right, start, stop):
                pe.matmul(out, left[0], right[0], start=start, stop=False)
                pe.matmul(out, left[0], right[1], start=False, stop=False)
                return pe.matmul(out, left[1], right[0], start=False, stop=stop)

            def split(t, half):
                pe.wait_ge(split_done, 2 * t + (half + 1 + SPLIT0))

            def part_of(par, col, n=P):
                return tuple(ring[:, par, part, col:col + n] for part in range(2))

            def h_part(k, a, b):
                return h_hi[:, k, a:b], h_lo[:, k, a:b]

            def project(par, t, chunks):
                for half in range(2):
                    split(t, half)
                    for k in range(4 * half, 4 * half + 4):
                        for a, b, o in chunks:
                            last = mm3(o, part_of(par, P * k), h_part(k, a, b), k == 0, k == KT - 1)
                    last.then_inc(slot_done, 1)

            def group_ends(shared, i, tile):
                return (not shared or i == 0 or tile == 0), (not shared or i == 0 or tile == 1)

            def project_pair(t, chunks, ready=None, between=None, shared=False, middle=None):
                for k in range(KT):
                    if k == 4 and middle is not None:
                        middle()
                    if k % 2 == 0:
                        split(t + k // 4 * (1 if middle is None else 3), k // 2 % 2)
                    if ready is not None:
                        pe.wait_ge(hlo_done, ready + k + 1)
                    for tile in range(2):
                        for i, (a, b, o) in enumerate(chunks[tile]):
                            opens, closes = group_ends(shared, i, tile)
                            last = mm3(o, part_of(k // 4, 2 * P * (k % 4) + P * tile),
                                       h_part(k, a, b), k == 0 and opens, k == KT - 1 and closes)
                    if k % 2:
                        last.then_inc(slot_done, 1)
                    if k == KT // 2 and between is not None:
                        between()

            def both_chunks(lat, ctx_out):
                return (0, LAT, lat), (LAT, TOK, ctx_out)

            def transform_weights(g, t):
                for r in range(KT):
                    if r % 4 == 0:
                        split(t + r // 4, 0)
                        split(t + r // 4, 1)
                    if r >= 4:
                        pe.wait_ge(wf_lo, KT * g + (r - 3))
                    for d in range(2):
                        last = mm3(bank(4 + r % 4, WCOLS), part_of(r // 4, 512 * d + P * (r % 4)),
                                   (feat[0][:, d, :], feat[1][:, d, :]), d == 0, d == 1)
                    last.then_inc(wf_mm, 1)
                    if r % 4 == 3:
                        pe.sem_inc(slot_done, 2)

            def ada_slot(c, q, t, par):
                for half in range(2):
                    split(t, half)
                    k = 2 * q + half
                    if k == 0:
                        pe.wait_ge(rows_done, c + 1)
                    for part in range(2):
                        last = pe.matmul(bank(7, parts=4), cond[:, k, :],
                                         ring[:, par, part, 512 * half:512 * half + 512],
                                         start=k == 0 and part == 0, stop=k == KT - 1 and part == 1)
                    last.then_inc(slot_done, 1)

            def turn_rows(c):
                pe.wait_ge(rows_done, c + 2)
                pe.wait_ge(mod_copied, c + 1)
                pe.sem_inc(turning, 1)
                for i in range(4):
                    last = pe.transpose(bank(6, 4, 4 * i), rows[:, P * i:P * i + P], ident4[:, :])
                last.then_inc(rows_tr, 1)

            pe.sem_inc(slot_done, DONE0)
            pe.sem_inc(rows_done, 1)
            pe.sem_inc(mod_copied, 1)
            pe.wait_ge(tab_lo, 1)
            transform_weights(0, 0)
            pe.wait_ge(tab_lo, 3)
            pe.wait_ge(cond_done, 2)
            pe.wait_ge(ident4_set, 2)
            for k in range(KT):
                if k >= 2:
                    pe.wait_ge(cosine_out, k - 1)
                    pe.wait_ge(sine_out, 3 * k - 3)
                b = 2 * (k % 2)

                def x_part(t):
                    return xs[0][:, t, P * k:P * k + P], xs[1][:, t, P * k:P * k + P]

                for out, table, t0, n in ((bank(b, NB), lat_cos, 0, 4),
                                          (bank(b + 1, LAT // 2), lat_sin, 0, 4),
                                          (bank(b + 1, CTX, LAT // 2), ctx_tab, 4, 2)):
                    for t in range(n):
                        if k == 0:
                            pe.wait_ge(xs_lo, t0 + t + 1)
                        last = mm3(out, x_part(t0 + t), (table[0][:, t, :], table[1][:, t, :]),
                                   t == 0, t == n - 1)
                last.then_inc(dft_done, 1)
                if k % 2 == 0 and k > 0:
                    turn_rows(k // 2 - 1)
                if k == 0:
                    pe.wait_ge(wf_lo, KT)
                for q in range(2):
                    ada_slot(k // 2, 2 * (k % 2) + q, SLOT_ADA0 + 2 * k + q, q)
            turn_rows(3)

            def fourier(g, first=False):
                pe.wait_ge(ds_done, 2 * g + 2)
                for k in range(KT):
                    pe.wait_ge(wf_lo, KT * g + (k + 1))
                    if first:
                        pe.wait_ge(hf_lo, 4 * k + 4)
                    for kind in range(2):
                        last = mm3(bank(kind, NF), tuple(w[:, k, P * kind:P * kind + P] for w in wf),
                                   (hf[0][kind][:, k, :], hf[1][kind][:, k, :]), k == 0, k == KT - 1)
                last.then_inc(u_done, 1)

            pe.wait_ge(shift_done, 5)
            pe.wait_ge(cosine_out, KT)
            pe.wait_ge(sine_out, 3 * KT)
            fourier(0, first=True)
            pe.wait_ge(mod_copied, 5)
            transform_weights(1, SLOT_U)
            pe.wait_ge(ones_set, 1)
            pe.wait_ge(diag_done, TT)
            for t in range(TT):
                last = pe.matmul(bank(2 + t // 4, P, P * (t % 4)), ones[:, :], diag[:, t, :],
                                 start=True, stop=True)
            last.then_inc(rstd_row_mm, 1)
            with pe.Fori(1, GROUPS - 1) as g:
                fourier(g)
                transform_weights(g + 1, 2 * g + SLOT_U)
            fourier(GROUPS - 1)
            pe.wait_ge(nyq_copied, 2 * GROUPS)
            pe.wait_ge(rstd_row, 1)
            for k in range(KT):
                last = mm3(bank(2, NF, parts=GROUPS), (nyq_w[0][:, k, :], nyq_w[1][:, k, :]),
                           (hf[0][0][:, k, :], hf[1][0][:, k, :]), k == 0, k == KT - 1)
            last.then_inc(nyq_mm, 1)

            def gates(jj, q, first=False, ready=None):
                j = 2 * jj + q
                t = Z_PER * j + SLOT_Z
                pe.wait_ge(z_done, 4 * j + 4)
                lat, ctx_out = (3 * q, 3 * q + 1), 3 * q + 2

                def adaln_half():
                    if not first:
                        turn_rows(j + 3)
                    ada_slot(j + 4, 0, t + 1, 1)
                    ada_slot(j + 4, 1, t + 2, 0)

                project_pair(t, [both_chunks(bank(lat[i]), bank(ctx_out, CTX, CTX * i))
                                 for i in range(2)], ready, shared=True, middle=adaln_half)
                ada_slot(j + 4, 2, t + 4, 0)
                ada_slot(j + 4, 3, t + 5, 1)

            pe.wait_ge(ds_done, 2 * GROUPS + 2)
            pe.wait_ge(nyq_vec, 1)
            gates(0, 0, first=True, ready=0)
            pe.wait_ge(wf_lo, KT * GROUPS)
            gates(0, 1)
            with pe.Fori(1, 4) as jj:
                gates(jj, 0)
                gates(jj, 1)

            def out_pair(t, chunks, g, ready, between=None, shared=False):
                for kk in range(FT):
                    if kk % 2 == 0:
                        split(t + kk // 4, kk // 2 % 2)
                    pe.wait_ge(glo, ready + kk + 1)
                    for tile in range(2):
                        for i, (a, b, o) in enumerate(chunks[tile]):
                            opens, closes = group_ends(shared, i, tile)
                            last = mm3(o, part_of(kk // 4 % 2, 2 * P * (kk % 4) + P * tile),
                                       (g(kk, 0)[:, a:b], g(kk, 1)[:, a:b]), kk == 0 and opens,
                                       kk == FT - 1 and closes)
                    if kk % 2:
                        last.then_inc(slot_done, 1)
                    if kk == 3 and between is not None:
                        between()

            def out_tile(t, chunks, g):
                for kk in range(FT):
                    if kk % 4 == 0:
                        split(t + kk // 8, kk // 4 % 2)
                    for a, b, o in chunks:
                        last = mm3(o, part_of(kk // 8, P * (kk % 8)),
                                   (g(kk, 0)[:, a:b], g(kk, 1)[:, a:b]), kk == 0, kk == FT - 1)
                    if kk % 4 == 3:
                        last.then_inc(slot_done, 1)

            pe.wait_ge(z_done, 4 * GROUPS + 4)
            out_pair(SLOT_OUT0, [both_chunks(bank(i), bank(2, CTX, CTX * i)) for i in range(2)],
                     g0, 0, between=lambda: turn_rows(CHUNKS - 1), shared=True)
            pe.wait_ge(z_done, 4 * GROUPS + 8)
            pe.wait_ge(mod_copied, CHUNKS + 1)
            for q in range(2):
                out_tile(SLOT_OUT0 + 4 + 2 * q, both_chunks(bank(3 + 2 * q), bank(4 + 2 * q, CTX)), g0)
            with pe.Fori(2, 4) as jj:
                for q in range(2):
                    pe.wait_ge(x1_done, 4 * jj + (2 * q + 2))
                    out_tile(4 * jj + (SLOT_OUT0 + 2 * q),
                             both_chunks(bank(3 + 2 * q), bank(4 + 2 * q, CTX)), g0)
            pe.wait_ge(acc_done, 2 * KT + 3)
            pe.matmul(bank(0), ones[:, :], acc_t[:, 0:LAT], start=True, stop=True).then_inc(sum_sq_done, 1)
            pe.wait_ge(acc_done, 2 * KT + 4)
            pe.matmul(bank(1, CTX), ones[:, :], acc_t[:, LAT:TOK], start=True,
                      stop=True).then_inc(sum_sq_done, 1)

            def o_sum(h):
                pe.wait_ge(oacc, 3 * h + 3)
                pe.matmul(bank(6), ones[:, :], head_rstd, start=True, stop=True).then_inc(oss, 1)

            def head(h, first=False):
                at = lambda s: HEAD_PER * h + (SLOT_HEAD + s)

                def lat(s, b):
                    project(s % 2, at(s), ((0, LAT, bank(b)),))

                def lat_pair(s, b0, b1, ready=None, between=None):
                    project_pair(at(s), [((0, LAT, bank(b0)),), ((0, LAT, bank(b1)),)], ready, between)

                if first:
                    pe.wait_ge(root_done, 2)
                    lat_pair(0, 0, 1, KT)
                else:
                    pe.wait_ge(vlo, 6 * h)
                    pe.wait_ge(z1_done, 4 * h)
                    pe.wait_ge(pf_done, 6 * h)
                    lat_pair(0, 0, 1, between=lambda: o_sum(h - 1))
                    pe.wait_ge(oroot, h)
                lat_pair(2, 7, 6)
                if first:
                    pe.wait_ge(hlo_done, 3 * KT)
                else:
                    pe.wait_ge(onorm, 4 * h)
                project_pair(at(4), [both_chunks(bank(2), bank(3, CTX)),
                                     both_chunks(bank(4), bank(5, CTX))])
                pe.wait_ge(z1_done, 4 * h + 1)
                lat(6, 7)
                pe.wait_ge(turned, 8 * h + 8)
                pe.wait_ge(qklo, 6 * h + 4)
                for s in range(7, 11):
                    for i in range(2):
                        split(at(s), i)
                        k = 2 * (s - 7) + i
                        for t in range(TT):
                            last = mm3(bank(V_BANK[t]), h_part(k, P * t, P * t + P),
                                       part_of(s % 2, DV * i, DV), k == 0, k == KT - 1)
                        last.then_inc(slot_done, 1)
                def scores(t):
                    if t < 2:
                        pe.wait_ge(z1_done, 4 * h + t + 2)
                    else:
                        pe.wait_ge(pf_done, 6 * h + t - 1)
                    for i in range(2):
                        last = mm3(bank(6 + t % 2),
                                   (k_s[0][:, i, P * t:P * t + P], k_s[1][:, i, P * t:P * t + P]),
                                   (q_s[0][:, i, :], q_s[1][:, i, :]), i == 0, i == 1)
                    last.then_inc(score_done, 1)

                pe.wait_ge(qklo, 6 * h + 6)
                scores(0)
                scores(1)
                pe.wait_ge(vlo, 6 * h + 1)
                lat(11, 0)
                for t in range(TT):
                    if t == 0:
                        pe.wait_ge(vlo, 6 * h + 5)
                    else:
                        pe.wait_ge(vlo, 6 * h + t + 1)
                    pe.wait_ge(plo, 6 * h + t + 1)
                    for i in range(4):
                        last = mm3(bank(2 + i),
                                   (v_s[0][:, t, P * i:P * i + P], v_s[1][:, t, P * i:P * i + P]),
                                   (p_s[0][:, t % 2, :], p_s[1][:, t % 2, :]), t == 0, t == TT - 1)
                    last.then_inc(pv_done, 1)
                    if t + 2 < TT:
                        scores(t + 2)

            head(0, first=True)
            with pe.Fori(1, HEADS) as h:
                head(h)

            pe.wait_ge(vlo, 6 * HEADS)
            pe.wait_ge(z1_done, 4 * HEADS)
            pe.wait_ge(pf_done, 6 * HEADS)
            out_pair(SLOT_OUT1, [((0, LAT, bank(i)),) for i in range(2)], g1, FT,
                     between=lambda: o_sum(HEADS - 1))
            pe.wait_ge(oroot, HEADS)
            for q in range(2):
                out_tile(SLOT_OUT1 + 4 + 2 * q, ((0, LAT, bank(7 - q)),), g1)
            with pe.Fori(2, 4) as jj:
                for q in range(2):
                    pe.wait_ge(x1_done, 2 * jj + (q + 2 * KT + 3))
                    out_tile(4 * jj + (SLOT_OUT1 + 2 * q), ((0, LAT, bank(7 - q)),), g1)
            pe.wait_ge(acc_done, 3 * KT + 5)
            pe.matmul(bank(0), ones[:, :], acc_t[:, 0:LAT], start=True, stop=True).then_inc(sum_sq_done, 1)


def mtile(w, cols):
    return w[:, cols].reshape(KT, P, P).transpose(1, 0, 2).reshape(P, SLOT)


def wide(w, first, k):
    return w[2 * P * k:2 * P * (k + 1), first:first + 512].reshape(2, P, 512).transpose(
        1, 0, 2).reshape(P, SLOT)


def pairs(w, rows, cols):
    part = w[rows][:, cols]
    return [part[4 * P * i:4 * P * (i + 1)].reshape(4, P, 2 * P).transpose(1, 0, 2).reshape(P, SLOT)
            for i in range(len(rows) // (4 * P))]


def weight_stream(ada_w, fnet_in, fnet_out, ret_in, ret_out):
    i = np.arange(P)
    all_rows = np.arange(D)
    feats = [np.concatenate([GDIM * g + i, GDIM * g + np.where(i == 0, P, GDIM - i)])
             for g in range(GROUPS)]

    def group(g):
        w = fnet_in[:, GDIM * g:GDIM * (g + 1)].T.reshape(2, P, 2, 512)
        return [w[:, :, s, :].transpose(1, 0, 2).reshape(P, SLOT) for s in range(2)]

    def ada(c):
        layer, first = c // 6, 512 * (c % 6)
        return [wide(ada_w[layer], first, k) for k in range(4)]

    slots = group(0)
    for c in range(4):
        slots += ada(c)
    for g in range(1, GROUPS):
        slots += group(g)
    for g in range(GROUPS):
        gates, rows = pairs(fnet_in, all_rows, DB + feats[g]), ada(4 + g)
        slots += gates[0:1] + rows[0:2] + gates[1:2] + rows[2:4]
    order = np.concatenate(feats)

    def output(w):
        found = pairs(w, np.arange(DB), np.arange(2 * P))
        for m in range(2, KT):
            for half in range(2):
                found.append(mtile(w[D * half:D * half + D], P * m + i))
        return found

    slots += output(fnet_out[order])
    quarter = QK // 4
    x1 = np.concatenate([np.arange(quarter), 2 * quarter + np.arange(quarter)])
    for h in range(HEADS):
        halves = np.concatenate([QK * h + x1, QK * h + x1 + quarter])
        z0 = 2 * D + DB + DV * h
        q = pairs(ret_in, all_rows, halves)
        k = pairs(ret_in, all_rows, D + halves)
        v = [wide(ret_in, 2 * D + DV * h, n) for n in range(4)]
        z01 = pairs(ret_in, all_rows, z0 + np.arange(2 * P))
        z23 = [mtile(ret_in, z0 + P * n + i) for n in (2, 3)]
        slots += q + z01 + k + z23[0:1] + v + z23[1:2]
    slots += output(ret_out)
    assert len(slots) == SLOTS
    return np.stack(slots)


def columns(v):
    return v.reshape(-1, P).T


def kernel(x, c, ctx, c_ctx, norm_g, ada_w, ada_b, fnet_w_in, fnet_w_out, ret_w_in, ret_w_out,
           ret_decay, final_g):
    import concourse.bacc as bacc
    from concourse.bass_utils import run_bass_kernel_spmd

    (x, c, ctx, c_ctx, norm_g, ada_w, ada_b, fnet_w_in, fnet_w_out, ret_w_in, ret_w_out, ret_decay,
     final_g) = (np.asarray(a) for a in (x, c, ctx, c_ctx, norm_g, ada_w, ada_b, fnet_w_in,
                                         fnet_w_out, ret_w_in, ret_w_out, ret_decay, final_g))

    def transposed(a):
        return a.T.reshape(KT, P, -1).transpose(1, 0, 2).reshape(P, -1)

    arrays = {
        "x_lat": transposed(x[0]),
        "x_ctx": transposed(ctx[0]),
        "x_rows": np.concatenate([x[0], ctx[0]], 0).reshape(TT, P, D),
        "small_in": np.concatenate([columns(c[0]), columns(c_ctx), columns(norm_g[0]),
                                    columns(norm_g[1]), columns(final_g), columns(ada_b[0]),
                                    columns(ada_b[1])], 1),
        "decay_in": ret_decay[0].reshape(8),
        "stream": weight_stream(ada_w, fnet_w_in[0], fnet_w_out[0], ret_w_in[0], ret_w_out[0]),
        "tables_in": dft_tables(),
        "rope_in": rope_tables(),
    }
    arrays = {n: np.ascontiguousarray(a) for n, a in arrays.items()}
    nc = bacc.Bacc("TRN2", target_bir_lowering=False, num_devices=1)
    args = [nc.dram_tensor(n, a.shape, F32, kind="ExternalInput").ap() for n, a in arrays.items()]
    out = nc.dram_tensor("out", (KT, P, LAT), F32, kind="ExternalOutput").ap()
    build(nc, *args, out)
    result = run_bass_kernel_spmd(nc, [arrays], core_ids=[0]).results[0]["out"]
    return result.reshape(D, LAT).T.reshape(1, LAT, D)
```
